# Optimizing a Trainium2 kernel written in Bass

```python
import math
import jax, jax.numpy as jnp
from jax import lax
import numpy as np

D_MODEL = 2048
BATCH = 1
SEQ = 256
DEPTH = 1
DEC_BATCH = 8
DEC_SEQ = 1
PAST_LEN = 2048
PAGE_SIZE = 128

D_MIX = D_MODEL
D_S5 = D_MIX // 2
D_M2 = D_MIX - D_S5
S5_CH = 16
S5_GROUPS = D_S5 // S5_CH
S5_N = 64
M2_HEADDIM = 64
M2_HEADS = D_M2 // M2_HEADDIM
M2_NGROUPS = 2
M2_DSTATE = 128
M2_CONV = 4
M2_CHUNK = 128
M2_CONV_DIM = D_M2 + 2 * M2_NGROUPS * M2_DSTATE
D_IN_PROJ = D_S5 + D_M2 + M2_CONV_DIM + M2_HEADS
MEM_LEN = 256
XA_HEADS = 4
XA_HEADDIM = D_MODEL // XA_HEADS
MOE_GROUPS = 4
MOE_PER_GROUP = 8
MOE_EXPERTS = MOE_GROUPS * MOE_PER_GROUP
MOE_TOPK = 2
MOE_FF = D_MODEL // 8
RMS_EPS = 1e-6

kernel_name = 'hymba_s5_ssd_hmoe_decode_step'

def rmsnorm(x, w):
    xf = x.astype(jnp.float32)
    y = xf * lax.rsqrt(jnp.mean(xf * xf, axis=-1, keepdims=True) + RMS_EPS)
    return (y * w.astype(jnp.float32)).astype(x.dtype)

def cplx_affine_combine(e1, e2):
    a1r, a1i, b1r, b1i = e1
    a2r, a2i, b2r, b2i = e2
    return (a2r * a1r - a2i * a1i,
            a2r * a1i + a2i * a1r,
            a2r * b1r - a2i * b1i + b2r,
            a2r * b1i + a2i * b1r + b2i)

def s5_branch(u, h0_re, h0_im, p):
    f32 = jnp.float32
    bsz, seq, _ = u.shape
    uf = u.astype(f32).reshape(bsz, seq, S5_GROUPS, S5_CH)
    lam_re = p['s5_a_re'].astype(f32)
    lam_im = p['s5_a_im'].astype(f32)
    step = jnp.exp(p['s5_log_dt'].astype(f32))[:, None]
    mag = jnp.exp(lam_re * step)
    ab_re = mag * jnp.cos(lam_im * step)
    ab_im = mag * jnp.sin(lam_im * step)
    den = lam_re * lam_re + lam_im * lam_im
    num_re = ab_re - 1.0
    coef_re = ((num_re * lam_re + ab_im * lam_im) / den)[..., None]
    coef_im = ((ab_im * lam_re - num_re * lam_im) / den)[..., None]
    b_re = p['s5_b_re'].astype(f32)
    b_im = p['s5_b_im'].astype(f32)
    bb_re = coef_re * b_re - coef_im * b_im
    bb_im = coef_re * b_im + coef_im * b_re
    bu_re = jnp.einsum('blgc,gnc->blgn', uf, bb_re)
    bu_im = jnp.einsum('blgc,gnc->blgn', uf, bb_im)
    a_re = jnp.broadcast_to(ab_re, bu_re.shape)
    a_im = jnp.broadcast_to(ab_im, bu_re.shape)
    pw_re, pw_im, h_re, h_im = lax.associative_scan(
        cplx_affine_combine, (a_re, a_im, bu_re, bu_im), axis=1)
    if h0_re is not None:
        s_re = h0_re.astype(f32)[:, None]
        s_im = h0_im.astype(f32)[:, None]
        h_re, h_im = (h_re + pw_re * s_re - pw_im * s_im,
                      h_im + pw_re * s_im + pw_im * s_re)
    c_re = p['s5_c_re'].astype(f32)
    c_im = p['s5_c_im'].astype(f32)
    y = jnp.einsum('gcn,blgn->blgc', c_re, h_re) - jnp.einsum('gcn,blgn->blgc', c_im, h_im)
    y = y.reshape(bsz, seq, D_S5) + p['s5_d'].astype(f32) * uf.reshape(bsz, seq, D_S5)
    g = jax.nn.gelu(y)
    out = g * jax.nn.sigmoid(g @ p['s5_glu_w'].astype(f32) + p['s5_glu_b'].astype(f32))
    out = rmsnorm(out, p['s5_norm_w'])
    return out.astype(u.dtype), h_re[:, -1], h_im[:, -1]

def causal_dwconv(xpad, w, b):
    y = lax.conv_general_dilated(
        xpad, w[:, None, :].astype(xpad.dtype), window_strides=(1,), padding='VALID',
        dimension_numbers=('NWC', 'WIO', 'NWC'), feature_group_count=xpad.shape[-1])
    return y + b.astype(y.dtype)

def ssd_chunked(x, dt, a, bmat, cmat):
    bsz, seq, nh, hp = x.shape
    q = M2_CHUNK
    nc = seq // q
    xdt = (x * dt[..., None]).reshape(bsz, nc, q, nh, hp)
    bc = bmat.reshape(bsz, nc, q, nh, M2_DSTATE)
    cc = cmat.reshape(bsz, nc, q, nh, M2_DSTATE)
    acum = jnp.cumsum((dt * a).reshape(bsz, nc, q, nh), axis=2)
    causal = jnp.tril(jnp.ones((q, q), dtype=bool))[None, None, :, :, None]
    seg = acum[:, :, :, None, :] - acum[:, :, None, :, :]
    lmat = jnp.exp(jnp.where(causal, seg, -jnp.inf))
    scores = jnp.einsum('bclhn,bcshn->bclsh', cc, bc) * lmat
    y_diag = jnp.einsum('bclsh,bcshp->bclhp', scores, xdt)
    decay_to_end = jnp.exp(acum[:, :, -1:, :] - acum)
    chunk_states = jnp.einsum('bcshn,bcsh,bcshp->bchpn', bc, decay_to_end, xdt)
    chunk_decay = jnp.exp(acum[:, :, -1, :])

    def pass_state(carry, inp):
        st, dec = inp
        return carry * dec[..., None, None] + st, carry

    init = jnp.zeros((bsz, nh, hp, M2_DSTATE), jnp.float32)
    final, prev = lax.scan(pass_state, init,
                           (jnp.swapaxes(chunk_states, 0, 1), jnp.swapaxes(chunk_decay, 0, 1)))
    prev = jnp.swapaxes(prev, 0, 1)
    y_off = jnp.einsum('bclhn,bchpn,bclh->bclhp', cc, prev, jnp.exp(acum))
    return (y_diag + y_off).reshape(bsz, seq, nh, hp), final

def ssd_recurrent(x, dt, a, bmat, cmat, h0):
    def step(h, inp):
        xt, dtt, bt, ct = inp
        h = h * jnp.exp(dtt * a)[..., None, None] + jnp.einsum('bhp,bhn->bhpn', xt * dtt[..., None], bt)
        return h, jnp.einsum('bhpn,bhn->bhp', h, ct)

    hT, ys = lax.scan(step, h0, (jnp.swapaxes(x, 0, 1), jnp.swapaxes(dt, 0, 1),
                                 jnp.swapaxes(bmat, 0, 1), jnp.swapaxes(cmat, 0, 1)))
    return jnp.swapaxes(ys, 0, 1), hT

def hybrid_mixer(xn, p, s5_state, ssm_state, conv_buf):
    f32 = jnp.float32
    bsz, seq, _ = xn.shape
    h = xn @ p['w_in']
    o1 = D_S5
    o2 = o1 + D_M2
    o3 = o2 + M2_CONV_DIM
    u, z, xbc, dt = h[..., :o1], h[..., o1:o2], h[..., o2:o3], h[..., o3:]
    if s5_state is None:
        s5_out, s5_re, s5_im = s5_branch(u, None, None, p)
    else:
        s5_out, s5_re, s5_im = s5_branch(u, s5_state[0], s5_state[1], p)
    if conv_buf is None:
        conv_buf = jnp.zeros((bsz, M2_CONV - 1, M2_CONV_DIM), xbc.dtype)
    xpad = jnp.concatenate([conv_buf.astype(xbc.dtype), xbc], axis=1)
    new_conv = xpad[:, -(M2_CONV - 1):]
    xbc = jax.nn.silu(causal_dwconv(xpad, p['m2_conv_w'], p['m2_conv_b']).astype(f32))
    nb = M2_NGROUPS * M2_DSTATE
    rep = M2_HEADS // M2_NGROUPS
    xs = xbc[..., :D_M2].reshape(bsz, seq, M2_HEADS, M2_HEADDIM)
    bmat = jnp.repeat(xbc[..., D_M2:D_M2 + nb].reshape(bsz, seq, M2_NGROUPS, M2_DSTATE), rep, axis=2)
    cmat = jnp.repeat(xbc[..., D_M2 + nb:].reshape(bsz, seq, M2_NGROUPS, M2_DSTATE), rep, axis=2)
    dtf = jax.nn.softplus(dt.astype(f32) + p['m2_dt_bias'].astype(f32))
    a = -jnp.exp(p['m2_a_log'].astype(f32))
    if ssm_state is None:
        y, ssm = ssd_chunked(xs, dtf, a, bmat, cmat)
    else:
        y, ssm = ssd_recurrent(xs, dtf, a, bmat, cmat, ssm_state.astype(f32))
    y = (y + p['m2_d'].astype(f32)[:, None] * xs).reshape(bsz, seq, D_M2)
    m2_out = rmsnorm(y * jax.nn.silu(z.astype(f32)), p['m2_norm_w']).astype(xn.dtype)
    out = jnp.concatenate([s5_out, m2_out], axis=-1) @ p['w_out']
    return out, s5_re, s5_im, ssm, new_conv

def memory_kv(mem, p):
    bsz = mem.shape[0]
    mn = rmsnorm(mem, p['norm_mem_w'])
    k = (mn @ p['xa_wk']).reshape(bsz, MEM_LEN, XA_HEADS, XA_HEADDIM)
    v = (mn @ p['xa_wv']).reshape(bsz, MEM_LEN, XA_HEADS, XA_HEADDIM)
    return k, v

def memory_cross_attention(xn, k, v, p):
    bsz, seq, _ = xn.shape
    q = (xn @ p['xa_wq']).reshape(bsz, seq, XA_HEADS, XA_HEADDIM)
    s = jnp.einsum('blhd,bmhd->bhlm', q.astype(jnp.float32), k.astype(jnp.float32)) * (XA_HEADDIM ** -0.5)
    att = jax.nn.softmax(s, axis=-1)
    o = jnp.einsum('bhlm,bmhd->blhd', att, v.astype(jnp.float32)).astype(xn.dtype)
    return o.reshape(bsz, seq, D_MODEL) @ p['xa_wo']

def hier_moe(xn, p):
    f32 = jnp.float32
    shp = xn.shape
    t = xn.reshape(-1, D_MODEL)
    tf = t.astype(f32)
    pc = jax.nn.softmax(tf @ p['router_coarse_w'].astype(f32) + p['router_coarse_b'].astype(f32), axis=-1)
    gsel = jnp.argmax(pc, axis=-1)
    gate_c = jnp.take_along_axis(pc, gsel[:, None], axis=-1)
    lf = (tf @ p['router_fine_w'].astype(f32) + p['router_fine_b'].astype(f32)).reshape(-1, MOE_GROUPS, MOE_PER_GROUP)
    lf_g = jnp.take_along_axis(lf, gsel[:, None, None], axis=1)[:, 0]
    top_l, top_i = lax.top_k(lf_g, MOE_TOPK)
    gate = jax.nn.softmax(top_l, axis=-1) * gate_c
    eidx = gsel[:, None] * MOE_PER_GROUP + top_i
    gates = jnp.sum(jax.nn.one_hot(eidx, MOE_EXPERTS, dtype=f32) * gate[..., None], axis=1)
    hg = jnp.einsum('td,edf->tef', t, p['moe_w_gate'])
    hu = jnp.einsum('td,edf->tef', t, p['moe_w_up'])
    hmid = jax.nn.silu(hg) * hu * gates[..., None].astype(hg.dtype)
    out = jnp.einsum('tef,efd->td', hmid, p['moe_w_down'])
    return out.reshape(shp).astype(xn.dtype)

def decoder_layer(x, mem_k, mem_v, p, s5_state, ssm_state, conv_buf):
    mix, s5_re, s5_im, ssm, conv = hybrid_mixer(rmsnorm(x, p['norm_mix_w']), p, s5_state, ssm_state, conv_buf)
    x = x + mix
    x = x + memory_cross_attention(rmsnorm(x, p['norm_xa_w']), mem_k, mem_v, p)
    x = x + hier_moe(rmsnorm(x, p['norm_ffn_w']), p)
    return x, s5_re, s5_im, ssm, conv

def setup_inputs(seed: int = 0) -> dict:
    key = jax.random.key(seed)
    ks = iter(jax.random.split(key, 64))
    f32 = jnp.float32

    def nrm(shape, scale=1.0):
        return scale * jax.random.normal(next(ks), shape, f32)

    def gain(shape):
        return 1.0 + 0.01 * nrm(shape)

    def unif(shape, lo, hi):
        return jax.random.uniform(next(ks), shape, f32, lo, hi)

    L = (DEPTH,)
    dt0 = jnp.exp(unif(L + (M2_HEADS,), math.log(1e-3), math.log(1e-1)))
    return {
        'x_prompt': nrm((BATCH, SEQ, D_MODEL)),
        'x_sample': nrm((DEC_BATCH, DEC_SEQ, D_MODEL)),
        'mem_prompt': nrm((BATCH, MEM_LEN, D_MODEL)),
        'state_s5_re': nrm(L + (DEC_BATCH, S5_GROUPS, S5_N), 0.1),
        'state_s5_im': nrm(L + (DEC_BATCH, S5_GROUPS, S5_N), 0.1),
        'state_ssm': nrm(L + (DEC_BATCH, M2_HEADS, M2_HEADDIM, M2_DSTATE), 0.1),
        'state_conv': nrm(L + (DEC_BATCH, M2_CONV - 1, M2_CONV_DIM)),
        'cache_mem_k': nrm(L + (DEC_BATCH, MEM_LEN, XA_HEADS, XA_HEADDIM)),
        'cache_mem_v': nrm(L + (DEC_BATCH, MEM_LEN, XA_HEADS, XA_HEADDIM)),
        'norm_mix_w': gain(L + (D_MODEL,)),
        'w_in': nrm(L + (D_MODEL, D_IN_PROJ), D_MODEL ** -0.5),
        's5_a_re': -0.5 + 0.01 * nrm(L + (S5_GROUPS, S5_N)),
        's5_a_im': jnp.pi * jnp.arange(S5_N, dtype=f32) + 0.01 * nrm(L + (S5_GROUPS, S5_N)),
        's5_log_dt': unif(L + (S5_GROUPS,), math.log(1e-3), math.log(1e-1)),
        's5_b_re': nrm(L + (S5_GROUPS, S5_N, S5_CH), (2 * S5_CH) ** -0.5),
        's5_b_im': nrm(L + (S5_GROUPS, S5_N, S5_CH), (2 * S5_CH) ** -0.5),
        's5_c_re': nrm(L + (S5_GROUPS, S5_CH, S5_N), S5_N ** -0.5),
        's5_c_im': nrm(L + (S5_GROUPS, S5_CH, S5_N), S5_N ** -0.5),
        's5_d': nrm(L + (D_S5,)),
        's5_glu_w': nrm(L + (D_S5, D_S5), D_S5 ** -0.5),
        's5_glu_b': nrm(L + (D_S5,), 0.01),
        's5_norm_w': gain(L + (D_S5,)),
        'm2_conv_w': nrm(L + (M2_CONV, M2_CONV_DIM), M2_CONV ** -0.5),
        'm2_conv_b': nrm(L + (M2_CONV_DIM,), 0.01),
        'm2_dt_bias': dt0 + jnp.log(-jnp.expm1(-dt0)),
        'm2_a_log': jnp.log(unif(L + (M2_HEADS,), 1.0, 16.0)),
        'm2_d': gain(L + (M2_HEADS,)),
        'm2_norm_w': gain(L + (D_M2,)),
        'w_out': nrm(L + (D_MIX, D_MODEL), D_MIX ** -0.5),
        'norm_xa_w': gain(L + (D_MODEL,)),
        'norm_mem_w': gain(L + (D_MODEL,)),
        'xa_wq': nrm(L + (D_MODEL, D_MODEL), D_MODEL ** -0.5),
        'xa_wk': nrm(L + (D_MODEL, D_MODEL), D_MODEL ** -0.5),
        'xa_wv': nrm(L + (D_MODEL, D_MODEL), D_MODEL ** -0.5),
        'xa_wo': nrm(L + (D_MODEL, D_MODEL), D_MODEL ** -0.5),
        'norm_ffn_w': gain(L + (D_MODEL,)),
        'router_coarse_w': nrm(L + (D_MODEL, MOE_GROUPS), D_MODEL ** -0.5),
        'router_coarse_b': nrm(L + (MOE_GROUPS,), 0.01),
        'router_fine_w': nrm(L + (D_MODEL, MOE_EXPERTS), D_MODEL ** -0.5),
        'router_fine_b': nrm(L + (MOE_EXPERTS,), 0.01),
        'moe_w_gate': nrm(L + (MOE_EXPERTS, D_MODEL, MOE_FF), D_MODEL ** -0.5),
        'moe_w_up': nrm(L + (MOE_EXPERTS, D_MODEL, MOE_FF), D_MODEL ** -0.5),
        'moe_w_down': nrm(L + (MOE_EXPERTS, MOE_FF, D_MODEL), MOE_FF ** -0.5),
        'norm_final_w': gain((D_MODEL,)),
    }

def reference(x_prompt, x_sample, mem_prompt, state_s5_re, state_s5_im, state_ssm, state_conv,
              cache_mem_k, cache_mem_v, norm_mix_w, w_in, s5_a_re, s5_a_im, s5_log_dt, s5_b_re, s5_b_im,
              s5_c_re, s5_c_im, s5_d, s5_glu_w, s5_glu_b, s5_norm_w, m2_conv_w, m2_conv_b, m2_dt_bias,
              m2_a_log, m2_d, m2_norm_w, w_out, norm_xa_w, norm_mem_w, xa_wq, xa_wk, xa_wv, xa_wo,
              norm_ffn_w, router_coarse_w, router_coarse_b, router_fine_w, router_fine_b,
              moe_w_gate, moe_w_up, moe_w_down, norm_final_w):
    yp, ys = x_prompt, x_sample
    lp = ([], [], [], [], [], [])
    ls = ([], [], [], [])
    for l in range(DEPTH):
        p = {
            'norm_mix_w': norm_mix_w[l], 'w_in': w_in[l],
            's5_a_re': s5_a_re[l], 's5_a_im': s5_a_im[l], 's5_log_dt': s5_log_dt[l],
            's5_b_re': s5_b_re[l], 's5_b_im': s5_b_im[l], 's5_c_re': s5_c_re[l], 's5_c_im': s5_c_im[l],
            's5_d': s5_d[l], 's5_glu_w': s5_glu_w[l], 's5_glu_b': s5_glu_b[l], 's5_norm_w': s5_norm_w[l],
            'm2_conv_w': m2_conv_w[l], 'm2_conv_b': m2_conv_b[l], 'm2_dt_bias': m2_dt_bias[l],
            'm2_a_log': m2_a_log[l], 'm2_d': m2_d[l], 'm2_norm_w': m2_norm_w[l], 'w_out': w_out[l],
            'norm_xa_w': norm_xa_w[l], 'norm_mem_w': norm_mem_w[l], 'xa_wq': xa_wq[l], 'xa_wk': xa_wk[l],
            'xa_wv': xa_wv[l], 'xa_wo': xa_wo[l], 'norm_ffn_w': norm_ffn_w[l],
            'router_coarse_w': router_coarse_w[l], 'router_coarse_b': router_coarse_b[l],
            'router_fine_w': router_fine_w[l], 'router_fine_b': router_fine_b[l],
            'moe_w_gate': moe_w_gate[l], 'moe_w_up': moe_w_up[l], 'moe_w_down': moe_w_down[l],
        }
        mk, mv = memory_kv(mem_prompt, p)
        yp, a1, a2, a3, a4 = decoder_layer(yp, mk, mv, p, None, None, None)
        for lst, arr in zip(lp, (a1, a2, a3, a4, mk, mv)):
            lst.append(arr)
        ys, b1, b2, b3, b4 = decoder_layer(ys, cache_mem_k[l], cache_mem_v[l], p,
                                           (state_s5_re[l], state_s5_im[l]), state_ssm[l], state_conv[l])
        for lst, arr in zip(ls, (b1, b2, b3, b4)):
            lst.append(arr)
    y_prompt = rmsnorm(yp, norm_final_w)
    y_sample = rmsnorm(ys, norm_final_w)
    p_s5_re = jnp.stack(lp[0])
    p_s5_im = jnp.stack(lp[1])
    p_ssm = jnp.stack(lp[2])
    p_conv = jnp.stack(lp[3])
    p_mem_k = jnp.stack(lp[4])
    p_mem_v = jnp.stack(lp[5])
    s_s5_re = jnp.stack(ls[0])
    s_s5_im = jnp.stack(ls[1])
    s_ssm = jnp.stack(ls[2])
    s_conv = jnp.stack(ls[3])
    return (y_prompt, y_sample, p_s5_re, p_s5_im, p_ssm, p_conv, p_mem_k, p_mem_v, s_s5_re, s_s5_im, s_ssm, s_conv)


_drawn_inputs = setup_inputs


def setup_inputs(seed=0):
    import zlib

    import numpy as np

    out = dict(_drawn_inputs(seed))
    spreads = {}
    factors = {'s5_a_re': 18.12,
     's5_glu_b': 8.0,
     's5_norm_w': 5.512,
     'm2_d': 64.0,
     'norm_xa_w': 8.0,
     'norm_mem_w': 5.528,
     'router_coarse_b': 31.672,
     'router_fine_b': 57.183,
     'norm_final_w': 31.935,
     'm2_conv_b': 3.173,
     'm2_norm_w': 7.227,
     'norm_ffn_w': 8.0}
    for name, (base, spread) in spreads.items():
        noise = np.random.default_rng([zlib.crc32(name.encode()), seed]).standard_normal(out[name].shape)
        drawn = base * np.exp(spread * noise) if base else spread * noise
        out[name] = __import__('jax').numpy.asarray(drawn.astype(out[name].dtype))
    for name, factor in factors.items():
        out[name] = (out[name] * factor).astype(out[name].dtype)
    return out
```

```python
from contextlib import ExitStack
import math

import concourse.bass as bass
from concourse import mybir

F32, I32 = mybir.dt.float32, mybir.dt.int32
ALU = mybir.AluOpType
ACT = mybir.ActivationFunctionType
AX = mybir.AxisListType

P = 128
D = 2048
KB = D // P
TP, TS = 256, 8
T = TP + TS
MEM = 256
HX, DX = 4, 512
EPS = 1e-6
ROUND = 12582912.0
ROUND14 = 768.0
TWO_PI = 6.2831850
INV_2PI = 0.15915494309189535
TWO_PI_PARTS = (6.28125, 1.93500518798828125e-3, 3.0199159819567e-7)
LOG2_E = 1.4426950408889634
LN_2_PARTS = (0.693359375, -2.12194440054690583e-4)
EXP_SERIES = tuple(1.0 / math.factorial(n) for n in range(8, -1, -1))
EXPERTS, FF = 32, 256
NS = 4
SLAB = 4096
GROUPS_X, EACH_X = 4, 8


def precise_exp(v, st, out, x, t, k):
    st(v.tensor_scalar(x, x, -87.0, 88.0, ALU.max, ALU.min))
    st(v.tensor_scalar(t, x, LOG2_E, ROUND, ALU.mult, ALU.add))
    st(v.tensor_scalar(t, t, ROUND, None, ALU.subtract))
    for part in LN_2_PARTS:
        st(v.scalar_tensor_tensor(x, t, -part, x, ALU.mult, ALU.add))
    st(v.tensor_scalar(t, t, 127.0, None, ALU.add))
    st(v.tensor_copy(k, t))
    st(v.tensor_scalar(k, k, 23, None, ALU.logical_shift_left))
    st(v.tensor_scalar(out, x, EXP_SERIES[0], EXP_SERIES[1], ALU.mult, ALU.add))
    for c in EXP_SERIES[2:]:
        st(v.tensor_tensor(out, out, x, ALU.mult))
        st(v.tensor_scalar(out, out, c, None, ALU.add))
    st(v.tensor_tensor(out, out, k.bitcast(F32), ALU.mult))


class Signal:

    every = []

    def __init__(self, sem):
        self.sem, self.base, self.n = sem, 0, 0
        Signal.every.append(self)

    def up(self, by=1):
        self.n += by
        return by

    def at(self, count):
        return self.base + count

    @staticmethod
    def stage():
        for s in Signal.every:
            s.base = s.n


def build(nc, I, O):
    Signal.every = []
    ctx = ExitStack()
    with ctx, nc.allow_non_contiguous_dma(reason="small parameters, loaded once"):
        def sb(name, shape, dt=F32):
            return ctx.enter_context(nc.sbuf_tensor(name, shape, dt))

        def signal(name):
            return Signal(ctx.enter_context(nc.semaphore(name)))

        ring = sb("ring", [P, NS, SLAB])
        XT = sb("XT", [P, KB, T])
        X = sb("X", [P, KB * T])
        H = sb("H", [P, 28 * T])
        M = sb("M", [P, 8192 + KB * T])
        S = sb("S", [P, 6144])
        par = sb("par", [P, 322])
        ident, ones, tri = (sb(n, [P, P]) for n in ("ident", "ones", "tri"))
        rstd = sb("rstd", [P, T])
        s5p = sb("s5p", [P, 7, 32])
        s5h = sb("s5h", [P, 2, TS, 32])
        wtmp = sb("wtmp", [P, 256])
        dtk = sb("dtk", [P, 3, 16])
        eps_c = sb("eps_c", [P, 2])
        ps = ctx.enter_context(nc.psum_tensor("ps", [P, 8, 512], F32))

        xn = X[:, :].rearrange("p (k t) -> p k t", t=T)
        h = H[:, :].rearrange("p (k t) -> p k t", t=T)
        u, z, xbc = h[:, 0:8, :], h[:, 8:16, :], h[:, 16:28, :]
        A = M[:, 8192:8192 + KB * T]
        memT = A[:, 0:KB * MEM].rearrange("p (k t) -> p k t", t=MEM)
        KT = M[:, 0:4096].rearrange("p (k t) -> p k t", t=MEM)
        V = M[:, 4096:8192].rearrange("p (a n) -> p a n", a=2)

        col = [0]

        def cols(n):
            col[0] += n
            assert col[0] <= 322
            return par[:, col[0] - n:col[0]]

        w_mix, w_mem, w_xa, w_ffn, w_fin = (cols(16) for _ in range(5))
        s5_dc, glu_bc, s5_wc, m2_wc, m2_dc = (cols(8) for _ in range(5))
        conv_wc = cols(48).rearrange("p (k c) -> p k c", k=4)
        conv_bc = cols(12)
        parity, half = cols(2), cols(2)
        dt_b, a_neg = cols(16), cols(16)
        mult = cols(32)
        tiny = cols(16)
        r_b = cols(36)

        steps = {n: signal(f"{n}_step") for n in ("act", "dve", "pool")}

        def stepper(eng, which):
            s = steps[which]

            def st(ins):
                ins.then_inc(s.sem, s.up())
                eng.wait_ge(s.sem, s.n)
                return ins
            return st

        slab_loaded = [signal(f"slab{i}_loaded") for i in range(NS)]
        slab_used, key_slab_used = signal("slab_used"), signal("key_slab_used")
        G, g = {}, 0
        for name, n in (("w_in", 14), ("xa_wk", 8), ("xa_wv", 8), ("glu", 2), ("w_out", 8), ("xa_wq", 8),
                        ("keys", 8), ("values", 8), ("xa_wo", 8), ("moe", 3 * EXPERTS)):
            G[name] = (g, n)
            g += n

        def used(g, more=0):
            first, n = G["keys"]
            if first <= g < first + n:
                return key_slab_used.sem, g - first + 1 + more
            return slab_used.sem, (g + 1 if g < first else g + 1 - n) + more

        def loaded(g, more=0):
            return slab_loaded[g % NS].sem, 16 * (g // NS + 1) + more

        def by_rows(w):
            return w.rearrange("(j p) n -> p j n", p=P)

        def slot(g):
            return ring[:, g % NS, :]

        def put_slab(sp, g):
            if g >= NS:
                sp.wait_ge(*used(g - NS))
            name = next(n for n, (f, c) in G.items() if f <= g < f + c)
            i = g - G[name][0]
            if name == "glu":
                dst = slot(g).rearrange("p (k n) -> p k n", n=512)
                src = by_rows(I["s5_glu_w"][0])[:, :, 512 * i:512 * i + 512]
            elif name in ("keys", "values"):
                dst = slot(g).rearrange("p (a n) -> p a n", a=2)
                src = I["cache_mem_k" if name == "keys" else "cache_mem_v"][0, i].rearrange(
                    "(a p) h d -> p a (h d)", p=P)
            elif name == "moe":
                return put_expert_slab(sp, g, i // 3, i % 3)
            else:
                dst = slot(g).rearrange("p (k n) -> p k n", n=256)
                src = by_rows(I[name][0])[:, :, 256 * i:256 * i + 256]
            sp.dma_start(dst, src).then_inc(slab_loaded[g % NS].sem, slab_loaded[g % NS].up(16))

        def expert_slab(e, which):
            if which < 2:
                w = I["moe_w_gate" if which == 0 else "moe_w_up"][0]
                return w[e].rearrange("(k p) n -> p k n", p=P) if isinstance(e, int) else \
                    w[bass.ds(e, 1)].rearrange("o (k p) n -> p (o k) n", p=P)
            w = I["moe_w_down"][0]
            return w[e].rearrange("(k p) n -> p k n", p=P) if isinstance(e, int) else \
                w[bass.ds(e, 1)].rearrange("o (k p) n -> p (o k) n", p=P)

        def slab_view(g, which):
            return slot(g).rearrange("p (k n) -> p k n", k=16 if which < 2 else 2)

        PAIR = [(0, 0), (0, 1), (1, 0), (1, 1), (0, 2), (1, 2)]

        def put_expert_slab(sp, g, *_):
            i = g - G["moe"][0]
            e, which = PAIR[i % 6]
            sp.dma_start(slab_view(g, which), expert_slab(2 * (i // 6) + e, which)).then_inc(slab_loaded[g % NS].sem, slab_loaded[g % NS].up(16))

        loaded_to = [0]

        def load_through(sp, end):
            for g in range(loaded_to[0], end):
                put_slab(sp, g)
            loaded_to[0] = end

        def load_matrix_loop(sp, name, end):
            first, n = G[name]
            g0 = loaded_to[0]
            i0 = g0 - first
            turns = (end - g0) // NS
            w = by_rows(I[name][0])
            with sp.Fori(0, turns) as it:
                for i in range(NS):
                    sp.wait_ge(*used(g0 + i - NS, it * NS))
                    src = w[:, :, bass.ds((it * NS + i0 + i) * 256, 256)]
                    sp.dma_start(slot(g0 + i).rearrange("p (k n) -> p k n", n=256), src).then_inc(
                        slab_loaded[(g0 + i) % NS].sem, 16)
            for i in range(NS):
                slab_loaded[i].n += 16 * turns
            loaded_to[0] = end

        block_done, block_taken = signal("output_block_done"), signal("output_block_taken")

        def project_pe(pe, name):
            first, n = G[name]

            def slab(i, it):
                pe.wait_ge(*loaded(first + i, 16 * it))
                w = slot(first + i).rearrange("p (k n) -> p k n", n=256)
                for o in range(2):
                    b = (2 * i + o) % 8
                    pe.wait_ge(block_taken.sem, block_taken.at(2 * i + o + 1 + 8 * it))
                    for k in range(KB):
                        mm = nc.tensor.matmul(ps[:, b, 0:T], w[:, k, o * P:(o + 1) * P], xn[:, k, :],
                                              start=(k == 0), stop=(k == KB - 1))
                        if k == KB - 1:
                            mm.then_inc((block_done if o == 0 else slab_used).sem, 1)

            with pe.Fori(0, n // 4) as it:
                for i in range(4):
                    slab(i, it)
            for i in range(n // 4 * 4, n):
                slab(i, 0)
            block_done.n += n
            slab_used.n += n

        def project_take(dve, name, take):
            first, n = G[name]

            def one(i, o, it):
                if o == 0:
                    dve.wait_ge(block_done.sem, block_done.at(i + 1 + 4 * it))
                else:
                    dve.wait_ge(*used(first + i, 4 * it))
                take(8 * it + 2 * i + o, (2 * i + o) % 8).then_inc(block_taken.sem, 1)

            with dve.Fori(0, n // 4) as it:
                for i in range(4):
                    for o in range(2):
                        one(i, o, it)
            for i in range(n // 4 * 4, n):
                for o in range(2):
                    one(i, o, 0)
            block_taken.n += 2 * n

        squares, sum_ready, root_ready, normed = (signal(s) for s in (
            "squares_ready", "square_sum_ready", "norm_root_ready", "normed_block_ready"))

        def norm_act(act, src, sq, nb, n, source=None, ahead=0):
            for k in range(nb):
                if source:
                    act.wait_ge(source.sem, source.at(k + 1 + ahead))
                nc.scalar.activation(sq[:, k, 0:n], src[:, k, 0:n], ACT.Square).then_inc(squares.sem, squares.up())
            act.wait_ge(sum_ready.sem, sum_ready.at(root_ready.n - root_ready.base + 1))
            nc.scalar.activation(rstd[:, 0:n], ps[:, 7, 0:n], ACT.Sqrt, scale=1.0 / (nb * P),
                                 bias=eps_c[:, 0:1]).then_inc(root_ready.sem, root_ready.up())

        def norm_pe(pe, sq, nb, n, before):
            for k in range(nb):
                pe.wait_ge(squares.sem, squares.at(before + k + 1))
                mm = nc.tensor.matmul(ps[:, 7, 0:n], ones[:, :], sq[:, k, 0:n], start=(k == 0), stop=(k == nb - 1))
            mm.then_inc(sum_ready.sem, sum_ready.up())

        def norm_dve(dve, src, dst, w, nb, n, nth):
            st = stepper(dve, "dve")
            dve.wait_ge(root_ready.sem, root_ready.at(nth))
            st(nc.vector.reciprocal(rstd[:, 0:n], rstd[:, 0:n]))
            for k in range(nb):
                nc.vector.scalar_tensor_tensor(dst[:, k, 0:n], src[:, k, 0:n], w[:, k:k + 1],
                                               rstd[:, 0:n], ALU.mult, ALU.mult).then_inc(normed.sem, normed.up())

        xrows = M[:, 0:6144].rearrange("p (a n) -> p a n", a=3)
        cwide = M[:, 6144:8192].rearrange("p (i q a n) -> p i q a n", i=2, q=8, a=2)
        braw = A[:, 0:1024].rearrange("p (i t c) -> p i t c", i=2, c=16)
        bbar = A[:, 1024:2048].rearrange("p (i t c) -> p i t c", i=2, c=16)
        bwide = A[:, 2048:4096].rearrange("p (i t a c) -> p i t a c", i=2, a=2, c=16)
        tabtmp = A[:, 0:1024].rearrange("p (t e) -> p t e", e=32)
        sq1 = H[:, 0:KB * T].rearrange("p (k t) -> p k t", t=T)
        btmp = H[:, 4224:4736].rearrange("p (t c) -> p t c", c=16)
        h0rows = X[:, 0:512].rearrange("p (i a n) -> p i a n", i=2, a=2)
        mult_i = X[:, 512:544].bitcast(I32)
        BT = S[:, 0:2048].rearrange("p (i q n) -> p i q n", i=2, q=8)
        CT = S[:, 2048:4096].rearrange("p (i q n) -> p i q n", i=2, q=8)
        cosT = S[:, 4096:5120].rearrange("p (t e) -> p t e", e=32)
        sinT = S[:, 5120:6144].rearrange("p (t e) -> p t e", e=32)
        MAG, TURN, COR, COI, AR, AI, NAI = range(7)
        rows32 = H[0:32, 4736:4736 + 16 * P].rearrange("t (r n) -> t r n", n=P)
        (lam_r, lam_i, dts, w2, w3, w4, w5, w6, r_mag, r_turn, r_cor, r_coi, r_ar, r_ai,
         r_nai) = (rows32[:, i, :] for i in range(15))

        const_ready, params_in, rows_in, s5_in = (signal(s) for s in (
            "constants_ready", "params_loaded", "input_rows_loaded", "s5_params_loaded"))
        tr_done, tr_taken = signal("transposes_done"), signal("transposes_taken")
        angle_ready, sine_ready = signal("angle_ready"), signal("sine_ready")
        rows_ready, wide_ready = signal("s5_rows_ready"), signal("s5_wide_ready")
        PARAMS = [("norm_mix_w", w_mix), ("norm_mem_w", w_mem), ("norm_xa_w", w_xa), ("norm_ffn_w", w_ffn),
                  ("s5_d", s5_dc), ("s5_glu_b", glu_bc), ("s5_norm_w", s5_wc), ("m2_norm_w", m2_wc),
                  ("m2_conv_b", conv_bc)]

        with nc.Block() as block:
            @block.sync
            def _(sp):
                sp.dma_start(xrows[:, 0:2, :], I["x_prompt"][0].rearrange("(a p) n -> p a n", p=P)).then_inc(rows_in.sem, rows_in.up(16))
                sp.dma_start(xrows[0:TS, 2, :], I["x_sample"].rearrange("b s n -> (b s) n")).then_inc(rows_in.sem, rows_in.up(16))
                load_through(sp, NS)

            @block.gpsimd
            def _(pool):
                st = stepper(pool, "pool")
                gp = nc.gpsimd
                gp.memset(ones[:, :], 1.0).then_inc(block_taken.sem, 8)
                st(gp.memset(ident[:, :], 0.0))
                gp.affine_select(out=ident[:, :], in_=ident[:, :], compare_op=ALU.not_equal,
                                 fill=1.0, base=0, pattern=[[-1, P]], channel_multiplier=1).then_inc(const_ready.sem, const_ready.up())
                st(gp.memset(tri[:, :], 1.0))
                st(gp.affine_select(out=tri[:, :], in_=tri[:, :], compare_op=ALU.is_ge, fill=0.0, base=0,
                                    pattern=[[1, P]], channel_multiplier=-1))
                st(gp.memset(eps_c[:, 0:1], EPS))
                st(gp.memset(eps_c[:, 1:2], 0.0))
                st(gp.memset(half, 1.0))
                st(gp.affine_select(out=half, in_=half, compare_op=ALU.is_ge, fill=0.0, base=0,
                                    pattern=[[-64, 2]], channel_multiplier=1))
                st(gp.affine_select(out=half, in_=half, compare_op=ALU.is_ge, fill=0.0, base=63,
                                    pattern=[[64, 2]], channel_multiplier=-1))
                st(gp.iota(mult_i[:, 0:16], pattern=[[1, 16]], base=0, channel_multiplier=0))
                st(gp.iota(mult_i[:, 16:32], pattern=[[16, 16]], base=0, channel_multiplier=0))
                st(gp.tensor_copy(mult, mult_i))
                pm = tiny[:, 0:8].rearrange("p (r a) -> p r a", a=2)
                st(gp.memset(pm, 1.0))
                st(gp.affine_select(out=pm, in_=pm, compare_op=ALU.is_ge, fill=0.0, base=0,
                                    pattern=[[-32, 4], [-16, 2]], channel_multiplier=1))
                st(gp.affine_select(out=pm, in_=pm, compare_op=ALU.is_ge, fill=0.0, base=15,
                                    pattern=[[32, 4], [16, 2]], channel_multiplier=-1))
                st(gp.tensor_tensor(tiny[:, 8:10], pm[:, 0, :], pm[:, 1, :], ALU.add))
                st(gp.tensor_tensor(tiny[:, 10:12], pm[:, 2, :], pm[:, 3, :], ALU.add))
                gp.tensor_tensor(parity, tiny[:, 8:10], tiny[:, 10:12], ALU.add).then_inc(const_ready.sem, const_ready.up())

            @block.scalar
            def _(act):
                def load(dst, src, s):
                    act.dma_start(dst, src).then_inc(s.sem, s.up(16))

                load(lam_r, I["s5_a_re"][0].rearrange("(t a) n -> t (a n)", a=2), s5_in)
                load(lam_i, I["s5_a_im"][0].rearrange("(t a) n -> t (a n)", a=2), s5_in)
                load(dts[:, 0:2], I["s5_log_dt"][0].rearrange("(t a) -> t a", a=2), s5_in)
                for i, name in enumerate(("s5_b_re", "s5_b_im")):
                    load(braw[:, i], I[name][0].rearrange("(t a) n c -> (a n) t c", a=2), s5_in)
                for i, name in enumerate(("s5_c_re", "s5_c_im")):
                    for a in range(2):
                        load(cwide[:, i, :, a, :], I[name][0].rearrange("(q e) c n -> (e c) q n", e=8), s5_in)
                for i, name in enumerate(("state_s5_re", "state_s5_im")):
                    load(h0rows[:, i], I[name][0].rearrange("(a b) (t g) n -> (b t) a (g n)", a=2, g=2), s5_in)
                for name, dst in PARAMS:
                    load(dst, I[name][0].rearrange("(k p) -> p k", p=P), params_in)
                load(w_fin, I["norm_final_w"].rearrange("(k p) -> p k", p=P), params_in)
                for k in range(4):
                    load(conv_wc[:, k, :], I["m2_conv_w"][0, k].rearrange("(c p) -> p c", p=P), params_in)
                for a in range(2):
                    load(m2_dc[64 * a:64 * a + 64, :],
                         I["m2_d"].rearrange("o (k a) -> o k a", a=2)[:, :, a].to_broadcast([64, 8]), params_in)
                load(dt_b, I["m2_dt_bias"].to_broadcast([P, 16]), params_in)
                load(a_neg, I["m2_a_log"].to_broadcast([P, 16]), params_in)
                load(r_b[:, 0:4], I["router_coarse_b"].to_broadcast([P, 4]), params_in)
                load(r_b[:, 4:36], I["router_fine_b"].to_broadcast([P, 32]), params_in)
                act.wait_ge(angle_ready.sem, angle_ready.at(1))
                act.wait_ge(const_ready.sem, const_ready.at(2))
                nc.scalar.activation(r_ai, w5, ACT.Sin, scale=TWO_PI, bias=eps_c[0:32, 1:2]).then_inc(sine_ready.sem, sine_ready.up())
                nc.scalar.activation(r_ar, w6, ACT.Sin, scale=TWO_PI, bias=eps_c[0:32, 1:2]).then_inc(sine_ready.sem, sine_ready.up())
                act.wait_ge(angle_ready.sem, angle_ready.at(2))
                nc.scalar.activation(sinT, sinT, ACT.Sin, scale=TWO_PI, bias=eps_c[:, 1:2]).then_inc(sine_ready.sem, sine_ready.up())
                nc.scalar.activation(cosT, cosT, ACT.Sin, scale=TWO_PI, bias=eps_c[:, 1:2]).then_inc(sine_ready.sem, sine_ready.up())
                norm_act(act, XT, sq1, KB, T, source=tr_taken)

            @block.vector
            def _(dve):
                st = stepper(dve, "dve")
                v = nc.vector
                for k in range(KB):
                    dve.wait_ge(tr_done.sem, tr_done.at(k + 1))
                    v.tensor_copy(XT[:, k, :], ps[:, k % 6, 0:T]).then_inc(tr_taken.sem, tr_taken.up())
                dve.wait_ge(s5_in.sem, s5_in.n)

                precise_exp(v, st, dts[:, 2:4], dts[:, 0:2], dts[:, 4:6], dts[:, 6:8].bitcast(I32))
                step = dts[:, 2:4].unsqueeze(2).to_broadcast([32, 2, 64])
                pairs = lambda a: a.rearrange("t (a n) -> t a n", a=2)
                st(v.tensor_tensor(pairs(w2), pairs(lam_r), step, ALU.mult))
                precise_exp(v, st, r_mag, w2, w3, w4.bitcast(I32))
                st(v.tensor_tensor(pairs(w3), pairs(lam_i), step, ALU.mult))
                st(v.tensor_scalar(w4, w3, INV_2PI, ROUND, ALU.mult, ALU.add))
                st(v.tensor_scalar(w4, w4, ROUND, None, ALU.subtract))
                for part in TWO_PI_PARTS:
                    st(v.scalar_tensor_tensor(w3, w4, -part, w3, ALU.mult, ALU.add))
                st(v.tensor_scalar(w5, w3, INV_2PI, None, ALU.mult))

                def wrap(x, t):
                    st(v.tensor_scalar(t, x, ROUND, None, ALU.add))
                    st(v.tensor_scalar(t, t, ROUND, None, ALU.subtract))
                    return v.tensor_tensor(x, x, t, ALU.subtract)

                st(wrap(w5, w4))
                st(v.tensor_copy(r_turn, w5))
                st(v.tensor_scalar(w6, w5, 0.25, None, ALU.add))
                wrap(w6, w4).then_inc(angle_ready.sem, angle_ready.up())
                dve.wait_ge(sine_ready.sem, sine_ready.at(2))
                st(v.tensor_tensor(r_ar, r_ar, r_mag, ALU.mult))
                st(v.tensor_tensor(r_ai, r_ai, r_mag, ALU.mult))
                st(v.tensor_scalar(r_nai, r_ai, -1.0, None, ALU.mult))
                st(v.tensor_scalar(w2, r_ar, -1.0, None, ALU.add))
                st(v.tensor_tensor(w3, lam_r, lam_r, ALU.mult))
                st(v.tensor_tensor(w4, lam_i, lam_i, ALU.mult))
                st(v.tensor_tensor(w3, w3, w4, ALU.add))
                st(v.reciprocal(w3, w3))
                st(v.tensor_tensor(r_cor, w2, lam_r, ALU.mult))
                st(v.tensor_tensor(w4, r_ai, lam_i, ALU.mult))
                st(v.tensor_tensor(r_cor, r_cor, w4, ALU.add))
                st(v.tensor_tensor(r_cor, r_cor, w3, ALU.mult))
                st(v.tensor_tensor(r_coi, r_ai, lam_r, ALU.mult))
                st(v.tensor_tensor(w4, w2, lam_i, ALU.mult))
                st(v.tensor_tensor(r_coi, r_coi, w4, ALU.subtract))
                v.tensor_tensor(r_coi, r_coi, w3, ALU.mult).then_inc(rows_ready.sem, rows_ready.up())
                dve.wait_ge(tr_done.sem, tr_done.at(KB + 1))
                st(v.tensor_copy(s5p[:, :, :], ps[:, 6, 0:224].rearrange("p (a t) -> p a t", t=32)))
                for i in range(2):
                    ins = v.tensor_copy(s5h[:, i].rearrange("p b t -> p (b t)"), ps[:, 4 + i, 0:256])
                    ins.then_inc(tr_taken.sem, tr_taken.up())
                per_c = lambda i: s5p[:, i, :].unsqueeze(2).to_broadcast([P, 32, 16])
                for i, (c1, c2, op) in enumerate(((COR, COI, ALU.subtract), (COI, COR, ALU.add))):
                    st(v.tensor_tensor(bbar[:, i], braw[:, 0], per_c(c1), ALU.mult))
                    st(v.tensor_tensor(btmp, braw[:, 1], per_c(c2), ALU.mult))
                    st(v.tensor_tensor(bbar[:, i], bbar[:, i], btmp, op))
                dve.wait_ge(const_ready.sem, const_ready.at(2))
                for i in range(2):
                    for a in range(2):
                        v.tensor_scalar(bwide[:, i, :, a, :], bbar[:, i], half[:, a:a + 1], None,
                                        ALU.mult).then_inc(wide_ready.sem, wide_ready.up())
                for i in range(2):
                    for a in range(2):
                        v.tensor_scalar(cwide[:, i, :, a, :], cwide[:, i, :, a, :],
                                        parity[:, a:a + 1], 1.0 - 2.0 * i, ALU.mult, ALU.mult).then_inc(wide_ready.sem, wide_ready.up())
                turn, high = s5p[:, TURN, :], s5p[:, COR, :]
                st(v.tensor_scalar(high, turn, ROUND14, None, ALU.add))
                st(v.tensor_scalar(high, high, ROUND14, None, ALU.subtract))
                st(v.tensor_tensor(turn, turn, high, ALU.subtract))
                per_e = lambda a: a.unsqueeze(2).to_broadcast([P, 32, 32])
                entries = mult.unsqueeze(1).to_broadcast([P, 32, 32])
                st(v.tensor_tensor(sinT, per_e(high), entries, ALU.mult))
                st(wrap(sinT, cosT))
                st(v.tensor_tensor(cosT, per_e(turn), entries, ALU.mult))
                st(v.tensor_tensor(sinT, sinT, cosT, ALU.add))
                st(wrap(sinT, cosT))
                st(v.tensor_scalar(cosT, sinT, 0.25, None, ALU.add))
                dve.wait_ge(wide_ready.sem, wide_ready.at(4))
                wrap(cosT, tabtmp).then_inc(angle_ready.sem, angle_ready.up())
                for n in range(8):
                    dst = (BT if n < 4 else CT)[:, n // 2 % 2, 4 * (n % 2):4 * (n % 2) + 4, :]
                    dve.wait_ge(tr_done.sem, tr_done.at(KB + 2 + n))
                    v.tensor_copy(dst, ps[:, n % 4, :].rearrange("p (q n) -> p q n", q=4)).then_inc(tr_taken.sem, tr_taken.up())
                dve.wait_ge(params_in.sem, params_in.n)
                norm_dve(dve, XT, xn, w_mix, KB, T, 1)

            @block.tensor
            def _(pe):
                pe.wait_ge(const_ready.sem, const_ready.at(2))
                pe.wait_ge(rows_in.sem, rows_in.at(32))
                for k in range(KB):
                    if k >= 6:
                        pe.wait_ge(tr_taken.sem, tr_taken.at(k - 5))
                    for a in range(2):
                        nc.tensor.transpose(ps[:, k % 6, a * P:(a + 1) * P], xrows[:, a, k * P:(k + 1) * P],
                                            ident[:, :])
                    nc.tensor.transpose(ps[:, k % 6, TP:T], xrows[0:TS, 2, k * P:(k + 1) * P],
                                        ident[0:TS, 0:TS]).then_inc(tr_done.sem, tr_done.up())
                pe.wait_ge(rows_ready.sem, rows_ready.at(1))
                pe.wait_ge(tr_taken.sem, tr_taken.at(KB))
                for i in range(2):
                    for a in range(2):
                        nc.tensor.transpose(ps[:, 4 + i, a * P:(a + 1) * P], h0rows[:, i, a, :], ident[:, :])
                for i, r in enumerate((r_mag, r_turn, r_cor, r_coi, r_ar, r_ai, r_nai)):
                    mm = nc.tensor.transpose(ps[:, 6, 32 * i:32 * i + 32], r, ident[0:32, 0:32])
                mm.then_inc(tr_done.sem, tr_done.up())
                for n in range(8):
                    i, q4 = n // 2 % 2, n % 2
                    pe.wait_ge(wide_ready.sem, wide_ready.at(4 if n < 4 else 8))
                    if n >= 4:
                        pe.wait_ge(tr_taken.sem, tr_taken.at(KB + 2 + n - 3))
                    for q in range(4 * q4, 4 * q4 + 4):
                        if n < 4:
                            src = bwide[:, i].rearrange("p t a c -> p (t a c)")[:, q * P:(q + 1) * P]
                        else:
                            src = cwide[:, i, q].rearrange("p a n -> p (a n)")
                        mm = nc.tensor.transpose(ps[:, n % 4, (q % 4) * P:(q % 4 + 1) * P], src, ident[:, :])
                    mm.then_inc(tr_done.sem, tr_done.up())
                norm_pe(pe, sq1, KB, T, 0)
        Signal.stage()

        dtw = M[:, 0:256].rearrange("p (k n) -> p k n", n=16)
        mrows = M[:, 4096:8192].rearrange("p (a n) -> p a n", a=2)
        sqm = X[:, 0:KB * MEM].rearrange("p (k t) -> p k t", t=MEM)
        dt_done = signal("time_step_sums_done")

        with nc.Block() as block:
            @block.sync
            def _(sp):
                sp.dma_start(mrows, I["mem_prompt"][0].rearrange("(a p) n -> p a n", p=P)).then_inc(rows_in.sem, rows_in.up(16))
                sp.dma_start(dtw, by_rows(I["w_in"][0])[:, :, 3584:3600]).then_inc(rows_in.sem, rows_in.up(16))
                load_matrix_loop(sp, "w_in", 12)
                load_through(sp, 18)

            @block.tensor
            def _(pe):
                project_pe(pe, "w_in")
                pe.wait_ge(block_taken.sem, block_taken.at(28 + 8))
                pe.wait_ge(rows_in.sem, rows_in.at(32))
                for a in range(3):
                    n = P if a < 2 else TS
                    for k in range(KB):
                        mm = nc.tensor.matmul(ps[0:n, 4, 16 * a:16 * a + 16], xn[:, k, a * P:a * P + n],
                                              dtw[:, k, :], start=(k == 0), stop=(k == KB - 1))
                mm.then_inc(dt_done.sem, dt_done.up())
                for k in range(KB):
                    if k >= 2:
                        pe.wait_ge(tr_taken.sem, tr_taken.at(k - 1))
                    for a in range(2):
                        mm = nc.tensor.transpose(ps[:, 5 + k % 2, a * P:(a + 1) * P],
                                                 mrows[:, a, k * P:(k + 1) * P], ident[:, :])
                    mm.then_inc(tr_done.sem, tr_done.up())
                norm_pe(pe, sqm, KB, MEM, 0)

            @block.vector
            def _(dve):
                st = stepper(dve, "dve")
                nc.vector.memset(dtk[:, :, :], 0.0)
                project_take(dve, "w_in", lambda k, b: nc.vector.tensor_copy(
                    h[:, bass.ds(k, 1), :], ps[:, b:b + 1, 0:T]))
                dve.wait_ge(dt_done.sem, dt_done.at(1))
                st(nc.vector.tensor_copy(dtk[:, 0:2, :], ps[:, 4, 0:32].rearrange("p (a n) -> p a n", a=2)))
                st(nc.vector.tensor_copy(dtk[0:TS, 2, :], ps[0:TS, 4, 32:48]))
                for k in range(KB):
                    dve.wait_ge(tr_done.sem, tr_done.at(k + 1))
                    nc.vector.tensor_copy(memT[:, k, :], ps[:, 5 + k % 2, 0:MEM]).then_inc(tr_taken.sem, tr_taken.up())
                norm_dve(dve, memT, memT, w_mem, KB, MEM, 1)

            @block.scalar
            def _(act):
                act.wait_ge(dt_done.sem, dt_done.at(1))
                norm_act(act, memT, sqm, KB, MEM, source=tr_taken)
        Signal.stage()

        srows = X[0:24, 0:1536]
        crows = X[0:11, 1536:3072]
        scT = X[:, 3072:3360].rearrange("p (c r) -> p c r", r=24)
        cv = X[:, 3360:3888].rearrange("p (s t) -> p s t", s=2)
        W = X[:, 0:1024].rearrange("p (s i t) -> p s i t", s=2, i=2)
        pr = X[:, 1024:2048].rearrange("p (j t) -> p j t", j=4)
        gin = X[:, 2048:2560].rearrange("p (i t) -> p i t", i=2)
        gsc = X[:, 2560:3072].rearrange("p (i t) -> p i t", i=2)
        hb = X[:, 3072:3072 + 4 * T].rearrange("p (s i t) -> p s i t", s=2, i=2)
        srow_out = X[:, 0:1024].rearrange("p (j n) -> p j n", n=P)
        conv_tr, conv_trt, conv_done, conv_free, conv_all = (signal(s) for s in (
            "conv_transposes_done", "conv_transposes_taken", "conv_block_done", "conv_block_activated",
            "conv_rows_stored"))
        raw_stored = signal("raw_rows_stored")
        kv_done, kv_taken, keys_tr, keys_tr_taken, kv_stored = (signal(s) for s in (
            "kv_block_done", "kv_block_taken", "keys_transposed", "keys_transpose_taken", "kv_stored"))
        rot_ready, rot_used, bu_done, bu_taken, state_ready, state_copied, y_done, y_q, y_taken = (
            signal(s) for s in ("rotation_ready", "rotation_used", "s5_inputs_done", "s5_inputs_taken",
                                "s5_states_ready", "s5_states_copied", "s5_outputs_done", "s5_output_block_done",
                                "s5_output_block_taken"))
        NT = 32

        with nc.Block() as block:
            @block.sync
            def _(sp):
                sp.dma_start(srows, I["state_conv"][0].rearrange("b r c -> (b r) c")).then_inc(rows_in.sem, rows_in.up(16))
                sp.dma_start(O["s_conv"][0][:, 0:2, :], I["state_conv"][0][:, 1:3, :]).then_inc(raw_stored.sem, raw_stored.up(16))
                sp.wait_ge(conv_trt.sem, conv_trt.at(4))
                sp.dma_start(O["p_conv"][0, 0], crows[0:3, :]).then_inc(raw_stored.sem, raw_stored.up(16))
                sp.dma_start(O["s_conv"][0][:, 2, :], crows[3:11, :]).then_inc(raw_stored.sem, raw_stored.up(16))
                sp.wait_ge(raw_stored.sem, raw_stored.at(48))
                for s in range(16):
                    g = G["xa_wk"][0] + s
                    if g + NS < 34:
                        load_through(sp, g + NS + 1)
                    sp.wait_ge(kv_taken.sem, kv_taken.at(s + 1))
                    out = O["p_mem_k" if s < 8 else "p_mem_v"][0, 0].rearrange("(a p) h d -> p a (h d)", p=P)
                    c = 256 * (s % 8)
                    sp.dma_start(out[:, :, c:c + 256], V[:, :, c:c + 256]).then_inc(kv_stored.sem, kv_stored.up(16))
                sp.wait_ge(kv_stored.sem, kv_stored.at(256))
                sp.wait_ge(conv_trt.sem, conv_trt.at(4 + 3))
                for i, (name, sname) in enumerate((("p_s5_re", "s_s5_re"), ("p_s5_im", "s_s5_im"))):
                    sp.dma_start(O[name][0, 0].rearrange("(t a) n -> t (a n)", a=2),
                                 srow_out[0:32, i, :]).then_inc(raw_stored.sem, raw_stored.up(16))
                    sp.dma_start(
          O[sname][0].rearrange("(a b) (t g) n -> (b t) a (g n)", a=2, g=2),
          srow_out[:, 2 + 2 * i:4 + 2 * i, :]).then_inc(raw_stored.sem, raw_stored.up(16))
                sp.wait_ge(raw_stored.sem, raw_stored.at(48 + 64))

            @block.tensor
            def _(pe):
                pe.wait_ge(rows_in.sem, rows_in.at(16))
                for c in range(12):
                    mm = nc.tensor.transpose(ps[:, 2, 24 * c:24 * c + 24], srows[:, c * P:(c + 1) * P],
                                             ident[0:24, 0:24])
                mm.then_inc(conv_tr.sem, conv_tr.up())
                for c in range(12):
                    mm = nc.tensor.transpose(ps[0:11, 3 + c // 4, (c % 4) * P:(c % 4 + 1) * P],
                                             xbc[:, c, TP - 3:T], ident[:, :])
                    if c % 4 == 3:
                        mm.then_inc(conv_tr.sem, conv_tr.up())

                def keys_values(s):
                    g = G["xa_wk"][0] + s
                    pe.wait_ge(*loaded(g))
                    if s >= 2:
                        pe.wait_ge(kv_taken.sem, kv_taken.at(s - 1))
                    w = slot(g).rearrange("p (k n) -> p k n", n=256)
                    for a in range(2):
                        for k in range(KB):
                            mm = nc.tensor.matmul(ps[:, s % 2, a * 256:(a + 1) * 256],
                                                  memT[:, k, a * P:(a + 1) * P], w[:, k, :],
                                                  start=(k == 0), stop=(k == KB - 1))
                    mm.then_inc(slab_used.sem, slab_used.up())

                def transpose_keys(s):
                    pe.wait_ge(kv_taken.sem, kv_taken.at(s + 1))
                    if s >= 1:
                        pe.wait_ge(keys_tr_taken.sem, keys_tr_taken.at(s))
                    else:
                        pe.wait_ge(conv_trt.sem, conv_trt.at(1))
                    for j in range(2):
                        for a in range(2):
                            mm = nc.tensor.transpose(ps[:, 2, j * 256 + a * P:j * 256 + (a + 1) * P],
                                                     V[:, a, s * 256 + j * P:s * 256 + (j + 1) * P], ident[:, :])
                    mm.then_inc(keys_tr.sem, keys_tr.up())

                def inputs(t):
                    q, r = t // 4, 32 * (t % 4)
                    if t >= 2:
                        pe.wait_ge(bu_taken.sem, bu_taken.at(t - 1))
                    elif t == 0:
                        pe.wait_ge(conv_trt.sem, conv_trt.at(4))
                    for i in range(2):
                        mm = nc.tensor.matmul(ps[:, 3 + 2 * (t % 2) + i, 0:T], BT[r:r + 32, i, q, :],
                                              u[r:r + 32, q, :], start=True, stop=True, tile_position=(r, 0))
                    mm.then_inc(bu_done.sem, bu_done.up())

                def outputs(t):
                    q, r = t // 4, 32 * (t % 4)
                    pe.wait_ge(state_ready.sem, state_ready.at(t + 1))
                    if t % 4 == 0 and t:
                        pe.wait_ge(y_taken.sem, y_taken.at(q))
                    for i in range(2):
                        mm = nc.tensor.matmul(ps[r:r + 32, 7, 0:T], CT[:, i, q, r:r + 32], hb[:, t % 2, i, :],
                                              start=(i == 0), stop=(i == 1), tile_position=(0, r))
                    mm.then_inc(y_done.sem, y_done.up())

                for s in range(16):
                    keys_values(s)
                    if 1 <= s <= 8:
                        transpose_keys(s - 1)
                    for t in (2 * s, 2 * s + 1):
                        if t >= 2:
                            outputs(t - 2)
                        inputs(t)
                outputs(30)
                outputs(31)
                pe.wait_ge(state_copied.sem, state_copied.at(4 * NT))
                pe.wait_ge(bu_taken.sem, bu_taken.at(NT))
                for i in range(2):
                    mm = nc.tensor.transpose(ps[0:32, 3, i * P:(i + 1) * P], s5p[:, TURN + i, :], ident[:, :])
                mm.then_inc(conv_tr.sem, conv_tr.up())
                for i in range(2):
                    for a in range(2):
                        mm = nc.tensor.transpose(
                            ps[:, 4 + i, a * P:(a + 1) * P],
                            s5h[:, i, 4 * a:4 * a + 4, :].rearrange("p b t -> p (b t)"), ident[:, :])
                    mm.then_inc(conv_tr.sem, conv_tr.up())

            @block.gpsimd
            def _(pool):
                st = stepper(pool, "pool")
                tt = nc.gpsimd.tensor_tensor
                pool.wait_ge(conv_free.sem, conv_free.at(12))
                for t in range(NT):
                    sq = lambda a: a.rearrange("p (a b) -> p a b", a=16)
                    cos, sin, tmp = sq(W[:, t % 2, 0, :]), sq(W[:, t % 2, 1, :]), sq(wtmp[:, :])
                    hi = lambda tab: tab[:, t, 16:32].unsqueeze(2).to_broadcast([P, 16, 16])
                    lo = lambda tab: tab[:, t, 0:16].unsqueeze(1).to_broadcast([P, 16, 16])
                    if t >= 2:
                        pool.wait_ge(rot_used.sem, rot_used.at(t - 1))
                    if t:
                        pool.wait_ge(rot_ready.sem, rot_ready.at(t))
                    tt(cos, hi(cosT), lo(cosT), ALU.mult)
                    tt(sin, hi(sinT), lo(cosT), ALU.mult)
                    st(tt(tmp, hi(sinT), lo(sinT), ALU.mult))
                    st(tt(cos, cos, tmp, ALU.subtract))
                    st(tt(tmp, hi(cosT), lo(sinT), ALU.mult))
                    tt(sin, sin, tmp, ALU.add).then_inc(rot_ready.sem, rot_ready.up())

            @block.vector
            def _(dve):
                st = stepper(dve, "dve")
                v = nc.vector
                tt, stt = v.tensor_tensor, v.scalar_tensor_tensor
                dve.wait_ge(conv_tr.sem, conv_tr.at(1))
                v.tensor_copy(scT.rearrange("p c r -> p (c r)"), ps[:, 2, 0:288]).then_inc(conv_trt.sem, conv_trt.up())
                for j in range(3):
                    dve.wait_ge(conv_tr.sem, conv_tr.at(2 + j))
                    v.tensor_copy(crows[:, 512 * j:512 * (j + 1)], ps[0:11, 3 + j, :]).then_inc(conv_trt.sem, conv_trt.up())
                dve.wait_ge(conv_trt.sem, conv_trt.at(1))
                for c in range(12):
                    o = cv[:, c % 2, :]
                    if c >= 2:
                        dve.wait_ge(conv_free.sem, conv_free.at(c - 1))
                    st(v.tensor_scalar(o, xbc[:, c, :], conv_wc[:, 3, c:c + 1], conv_bc[:, c:c + 1],
                                       ALU.mult, ALU.add))
                    for k in range(3):
                        s = 3 - k
                        stt(o[:, TP:T], scT[:, c, :].rearrange("p (b r) -> p r b", r=3)[:, k, :],
                            conv_wc[:, k, c:c + 1], o[:, TP:T], ALU.mult, ALU.add)
                        ins = stt(o[:, s:TP], xbc[:, c, 0:TP - s], conv_wc[:, k, c:c + 1], o[:, s:TP],
                                  ALU.mult, ALU.add)
                        if k < 2:
                            st(ins)
                    ins.then_inc(conv_done.sem, conv_done.up())
                dve.wait_ge(conv_free.sem, conv_free.at(12))
                dve.wait_ge(raw_stored.sem, raw_stored.at(48))
                for t in range(NT):
                    q = t // 4
                    br, bi = (ps[:, 3 + 2 * (t % 2) + i, :] for i in range(2))
                    cos, sin = W[:, t % 2, 0, :], W[:, t % 2, 1, :]
                    sc = lambda j: s5p[:, j, t:t + 1]
                    hr, hi = hb[:, t % 2, 0, :], hb[:, t % 2, 1, :]
                    dve.wait_ge(rot_ready.sem, rot_ready.at(t + 1))
                    dve.wait_ge(bu_done.sem, bu_done.at(t + 1))
                    if t:
                        dve.wait_ge(state_ready.sem, state_ready.at(t))
                    if t >= 2:
                        dve.wait_ge(y_done.sem, y_done.at(t - 1))
                        dve.wait_ge(state_copied.sem, state_copied.at(4 * (t - 1)))
                    tt(pr[:, 0], br[:, 0:TP], cos, ALU.mult)
                    tt(pr[:, 1], bi[:, 0:TP], sin, ALU.mult)
                    tt(pr[:, 2], bi[:, 0:TP], cos, ALU.mult)
                    stt(hr[:, TP:T], s5h[:, 0, :, t], sc(AR), br[:, TP:T], ALU.mult, ALU.add)
                    stt(hi[:, TP:T], s5h[:, 1, :, t], sc(AR), bi[:, TP:T], ALU.mult, ALU.add)
                    tt(pr[:, 3], br[:, 0:TP], sin, ALU.mult).then_inc(bu_taken.sem, bu_taken.up())
                    dve.wait_ge(bu_taken.sem, bu_taken.at(t + 1))
                    tt(gin[:, 0], pr[:, 0], pr[:, 1], ALU.add)
                    stt(hr[:, TP:T], s5h[:, 1, :, t], sc(NAI), hr[:, TP:T], ALU.mult, ALU.add)
                    stt(hi[:, TP:T], s5h[:, 0, :, t], sc(AI), hi[:, TP:T], ALU.mult, ALU.add)
                    st(tt(gin[:, 1], pr[:, 2], pr[:, 3], ALU.subtract))
                    mag = sc(MAG).to_broadcast([P, TP])
                    v.tensor_tensor_scan(gsc[:, 0], mag, gin[:, 0], 0.0, ALU.mult, ALU.add)
                    st(v.tensor_tensor_scan(gsc[:, 1], mag, gin[:, 1], 0.0, ALU.mult, ALU.add))
                    tt(pr[:, 0], gsc[:, 0], cos, ALU.mult)
                    tt(pr[:, 1], gsc[:, 1], sin, ALU.mult)
                    tt(pr[:, 2], gsc[:, 1], cos, ALU.mult)
                    tt(pr[:, 3], gsc[:, 0], sin, ALU.mult).then_inc(rot_used.sem, rot_used.up())
                    dve.wait_ge(rot_used.sem, rot_used.at(t + 1))
                    tt(hr[:, 0:TP], pr[:, 0], pr[:, 1], ALU.subtract)
                    tt(hi[:, 0:TP], pr[:, 2], pr[:, 3], ALU.add).then_inc(state_ready.sem, state_ready.up())
                    if t % 4 == 1 and t > 4:
                        dve.wait_ge(y_done.sem, y_done.at(4 * (q - 1) + 4))
                        stt(u[:, q - 1, :], u[:, q - 1, :], s5_dc[:, q - 1:q], ps[:, 7, 0:T],
                            ALU.mult, ALU.add).then_inc(y_taken.sem, y_taken.up())
                dve.wait_ge(y_done.sem, y_done.at(NT))
                stt(u[:, 7, :], u[:, 7, :], s5_dc[:, 7:8], ps[:, 7, 0:T], ALU.mult, ALU.add).then_inc(y_taken.sem, y_taken.up())
                dve.wait_ge(conv_tr.sem, conv_tr.at(5))
                v.tensor_copy(srow_out[0:32, 0:2, :],
                              ps[0:32, 3, 0:256].rearrange("p (j n) -> p j n", n=P)).then_inc(conv_trt.sem, conv_trt.up())
                for i in range(2):
                    dve.wait_ge(conv_tr.sem, conv_tr.at(6 + i))
                    v.tensor_copy(srow_out[:, 2 + 2 * i:4 + 2 * i, :],
                                  ps[:, 4 + i, 0:256].rearrange("p (j n) -> p j n", n=P)).then_inc(conv_trt.sem, conv_trt.up())

            @block.scalar
            def _(act):
                def take_kv(s):
                    act.wait_ge(*used(G["xa_wk"][0] + s))
                    if s == 8:
                        act.wait_ge(kv_stored.sem, kv_stored.at(128))
                        act.wait_ge(keys_tr_taken.sem, keys_tr_taken.at(8))
                    c = 256 * (s % 8)
                    nc.scalar.copy(V[:, :, c:c + 256],
                                   ps[:, s % 2, :].rearrange("p (a n) -> p a n", a=2)).then_inc(kv_taken.sem, kv_taken.up())

                def take_keys(s):
                    act.wait_ge(keys_tr.sem, keys_tr.at(s + 1))
                    nc.scalar.copy(
       KT[:, 2 * s:2 * s + 2, :].rearrange("p k t -> p (k t)"), ps[:, 2, :]).then_inc(keys_tr_taken.sem, keys_tr_taken.up())

                def copy_states(t):
                    act.wait_ge(state_ready.sem, state_ready.at(t + 1))
                    for i in range(2):
                        src = hb[:, t % 2, i, :]
                        nc.scalar.copy(s5p[:, TURN + i, t:t + 1], src[:, TP - 1:TP]).then_inc(state_copied.sem, state_copied.up())
                        nc.scalar.copy(s5h[:, i, :, t], src[:, TP:T]).then_inc(state_copied.sem, state_copied.up())

                for c in range(12):
                    act.wait_ge(conv_done.sem, conv_done.at(c + 1))
                    nc.scalar.activation(xbc[:, c, :], cv[:, c % 2, :], ACT.Silu).then_inc(conv_free.sem, conv_free.up())
                for k in range(8):
                    nc.scalar.activation(z[:, k, :], z[:, k, :], ACT.Silu)
                for s in range(16):
                    if s == 8:
                        take_keys(7)
                    take_kv(s)
                    if 1 <= s <= 7:
                        take_keys(s - 1)
                    if s >= 1:
                        copy_states(2 * s - 2)
                        copy_states(2 * s - 1)
                copy_states(30)
                copy_states(31)
        Signal.stage()

        xdt = S[:, 0:2048].rearrange("p (c n) -> p c n", c=2)
        xw = S[:, 2048:4096].rearrange("p (c n) -> p c n", c=2)
        Gm = S[:, 4096:4608].rearrange("p (j l) -> p j l", j=4)
        Btok = S[:, 4608:5120].rearrange("p (j n) -> p j n", j=4)
        S0 = S[:, 5120:6144]
        seg = X[:, 0:1024].rearrange("p (s j) -> p s j", s=2)
        Mt = X[:, 1024:2048].rearrange("p (s j) -> p s j", s=2)
        rowexp = X[:, 2048:3072].rearrange("p (s j) -> p s j", s=2)
        CE = X[:, 3072:4096].rearrange("p (s j) -> p s j", s=2)
        fin, fout = A[:, 0:1024], A[:, 1024:2048]
        wide_dt = A[0:TS, 0:2048].rearrange("b (i n) -> b i n", i=2)
        hs = A[:, 2048:4096].rearrange("p (s k n) -> p s k n", s=2, n=P)
        dexp = A[:, 4096:4224].rearrange("p (k i b) -> p k i b", k=8, i=2)
        da = wtmp[:, 0:48].rearrange("p (a n) -> p a n", a=3)
        acum = wtmp[:, 48:80].rearrange("p (c n) -> p c n", c=2)
        dend = wtmp[:, 80:112].rearrange("p (c n) -> p c n", c=2)
        cdec = wtmp[:, 112:144].rearrange("p (c n) -> p c n", c=2)
        xds = wtmp[:, 144:208].rearrange("p (k b) -> p k b", k=8)
        ys = s5p[:, 0:2, :].rearrange("p a b -> p (a b)").rearrange("p (k b) -> p k b", k=8)
        small = s5h[:, :, :, :].rearrange("p a b c -> p (a b c)")
        sp_x, sp_e, sp_t, sp_k, sp_s = (small[:, 48 * i:48 * i + 48] for i in range(5))
        junk = small[:, 256:384]
        (ssd_in, xtok_done, xtok_taken, btok_taken, gm_taken, da_ready, cum_done, cum_taken, ends_ready,
         xw_ready, st_done, st_taken, row_done, seg_ready, seg_exp, m_ready, ysd_done, ysd_taken, fin_tr,
         fin_taken) = (signal(f"ssd_{n}") for n in (
             "loaded", "x_rows_done", "x_rows_taken", "b_rows_taken", "gram_taken", "decay_rates_ready",
             "cumulated", "cumulated_taken", "decay_to_end_ready", "weighted_x_ready", "state_done",
             "state_taken", "row_decay_done", "segment_ready", "segment_exp_ready", "masked_ready",
             "y_done", "y_taken", "final_transposed", "final_taken"))
        (spread_done, spread_taken, carried_scaled, bc_done, bc_taken) = (
            signal(f"sample_{n}") for n in (
                "decays_spread", "spread_taken", "state_decayed", "bc_rows_done", "bc_rows_taken"))
        carried_in = [signal(f"sample_state_loaded{i}") for i in range(2)]
        carried_out = [signal(f"sample_state_stored{i}") for i in range(2)]

        with nc.Block() as block:
            @block.sync
            def _(sp):
                state = I["state_ssm"][0].rearrange("b (k a) p n -> b (a p) k n", a=2)
                out = O["s_ssm"][0].rearrange("b (k a) p n -> b (a p) k n", a=2)
                for b in range(TS + 2):
                    if b < TS:
                        if b >= 2:
                            sp.wait_ge(carried_out[b % 2].sem, carried_out[b % 2].at(16 * (b // 2)))
                        sp.dma_start(hs[:, b % 2], state[b]).then_inc(carried_in[b % 2].sem, carried_in[b % 2].up(16))
                    if 1 <= b <= TS:
                        sp.wait_ge(bc_taken.sem, bc_taken.at(b))
                        sp.dma_start(out[b - 1], hs[:, (b - 1) % 2]).then_inc(carried_out[(b - 1) % 2].sem, carried_out[(b - 1) % 2].up(16))
                sp.wait_ge(fin_taken.sem, fin_taken.at(2))
                sp.dma_start(
  O["p_ssm"][0, 0].rearrange("(k a) p n -> (a p) k n", a=2),
  fout.rearrange("p (k n) -> p k n", n=P)).then_inc(carried_out[0].sem, carried_out[0].up(16))
                sp.wait_ge(carried_out[0].sem, carried_out[0].at(16 * 5))
                sp.wait_ge(carried_out[1].sem, carried_out[1].at(16 * 4))

            @block.tensor
            def _(pe):
                for n in range(4):
                    c, j = n // 2, n % 2
                    for k in range(4):
                        mm = nc.tensor.transpose(ps[:, n, k * P:(k + 1) * P],
                                                 xbc[:, 4 * j + k, c * P:(c + 1) * P], ident[:, :])
                    mm.then_inc(xtok_done.sem, xtok_done.up())
                for n in range(4):
                    c, g = n // 2, n % 2
                    mm = nc.tensor.transpose(ps[:, 4, n * P:(n + 1) * P], xbc[:, 8 + g, c * P:(c + 1) * P],
                                             ident[:, :])
                mm.then_inc(xtok_done.sem, xtok_done.up())
                for n in range(4):
                    c, g = n // 2, n % 2
                    mm = nc.tensor.matmul(ps[:, 5, n * P:(n + 1) * P], xbc[:, 8 + g, c * P:(c + 1) * P],
                                          xbc[:, 10 + g, c * P:(c + 1) * P], start=True, stop=True)
                mm.then_inc(xtok_done.sem, xtok_done.up())
                pe.wait_ge(da_ready.sem, da_ready.at(1))
                for c in range(2):
                    nc.tensor.matmul(ps[:, 6, 16 * c:16 * c + 16], tri[:, :], da[:, c, :], start=True, stop=True)
                    mm = nc.tensor.matmul(ps[:, 6, 32 + 16 * c:48 + 16 * c], ones[:, :], da[:, c, :],
                                          start=True, stop=True)
                mm.then_inc(cum_done.sem, cum_done.up())
                pe.wait_ge(da_ready.sem, da_ready.at(3))
                for k in range(8):
                    for i in range(2):
                        mm = nc.tensor.transpose(ps[:, 7, 16 * k + 8 * i:16 * k + 8 * i + 8],
                                                 wide_dt[:, i, k * P:(k + 1) * P], ident[0:TS, 0:TS])
                mm.then_inc(spread_done.sem, spread_done.up())
                pe.wait_ge(xw_ready.sem, xw_ready.at(4))
                pe.wait_ge(btok_taken.sem, btok_taken.at(1))
                for n in range(4):
                    c, g = n // 2, n % 2
                    nc.tensor.matmul(ps[:, n, :], Btok[:, n, :], xw[:, c, 512 * g:512 * g + 512],
                                     start=True, stop=True).then_inc(st_done.sem, st_done.up())

                def row_decay(n):
                    c, qd = n // 4, n % 4
                    if n < 2:
                        pe.wait_ge(gm_taken.sem, gm_taken.at(1))
                    else:
                        pe.wait_ge(seg_ready.sem, seg_ready.at(n - 1))
                        if n - 2 >= 4:
                            pe.wait_ge(seg_exp.sem, seg_exp.at((n - 2) + (n - 2 - 4) + 1))
                    for j in range(4):
                        mm = nc.tensor.matmul(ps[:, 4 + n % 2, j * P:(j + 1) * P],
                                              da[:, c, 4 * qd + j:4 * qd + j + 1].to_broadcast([P, P]), tri[:, :],
                                              start=True, stop=True)
                    mm.then_inc(row_done.sem, row_done.up())

                def y_out(n):
                    c, qd = n // 4, n % 4
                    pe.wait_ge(m_ready.sem, m_ready.at(n + 1))
                    if n < 2:
                        pe.wait_ge(cum_taken.sem, cum_taken.at(1))
                        if n == 1:
                            pe.wait_ge(spread_taken.sem, spread_taken.at(1))
                    else:
                        pe.wait_ge(ysd_taken.sem, ysd_taken.at(2 * (n - 1)))
                    if c:
                        pe.wait_ge(st_taken.sem, st_taken.at(2))
                    for j in range(4):
                        hd = 4 * qd + j
                        o = ps[64 * (hd % 2):64 * (hd % 2) + 64, 6 + n % 2, (j // 2) * P:(j // 2 + 1) * P]
                        mm = nc.tensor.matmul(o, xdt[:, c, 64 * hd:64 * hd + 64], Mt[:, n % 2, j * P:(j + 1) * P],
                                              start=True, stop=(c == 0), tile_position=(0, 64 * (hd % 2)))
                        if c:
                            mm = nc.tensor.matmul(o, S0[:, 64 * hd:64 * hd + 64], CE[:, n % 2, j * P:(j + 1) * P],
                                                  start=False, stop=True, tile_position=(0, 64 * (hd % 2)))
                    mm.then_inc(ysd_done.sem, ysd_done.up())

                row_decay(0)
                row_decay(1)
                for n in range(8):
                    y_out(n)
                    if n + 2 < 8:
                        row_decay(n + 2)
                pe.wait_ge(st_taken.sem, st_taken.at(4))
                for k in range(8):
                    mm = nc.tensor.transpose(ps[:, k // 4, (k % 4) * P:(k % 4 + 1) * P], fin[:, k * P:(k + 1) * P],
                                             ident[:, :])
                    if k % 4 == 3:
                        mm.then_inc(fin_tr.sem, fin_tr.up())
                for b in range(TS):
                    if b >= 2:
                        pe.wait_ge(bc_taken.sem, bc_taken.at(b - 1))
                    for j in range(4):
                        mm = nc.tensor.matmul(ps[:, 2 + b % 2, j * P:(j + 1) * P],
                                              xbc[:, 8 + j, TP + b:TP + b + 1].to_broadcast([P, P]), ident[:, :],
                                              start=True, stop=True)
                    mm.then_inc(bc_done.sem, bc_done.up())

            @block.vector
            def _(dve):
                st = stepper(dve, "dve")
                v = nc.vector
                tt, stt, ts = v.tensor_tensor, v.scalar_tensor_tensor, v.tensor_scalar
                flat = dtk[:, :, :].rearrange("p a n -> p (a n)")
                st(tt(sp_x.rearrange("p (a n) -> p a n", a=3), dtk[:, :, :],
                      dt_b.unsqueeze(1).to_broadcast([P, 3, 16]), ALU.add))
                st(stt(sp_e, sp_x, -1.0, sp_x, ALU.mult, ALU.min))
                precise_exp(v, st, sp_s, sp_e, sp_t, sp_k.bitcast(I32))
                st(ts(sp_t, sp_s, 2.0, None, ALU.add))
                st(v.reciprocal(sp_t, sp_t))
                st(tt(sp_s, sp_s, sp_t, ALU.mult))
                st(tt(sp_e, sp_s, sp_s, ALU.mult))
                st(ts(sp_t, sp_e, 1.0 / 17, 1.0 / 15, ALU.mult, ALU.add))
                for c in (13, 11, 9, 7, 5, 3, 1):
                    st(tt(sp_t, sp_t, sp_e, ALU.mult))
                    st(ts(sp_t, sp_t, 1.0 / c, None, ALU.add))
                st(stt(sp_t, sp_t, 2.0, sp_s, ALU.mult, ALU.mult))
                st(stt(flat, sp_x, 0.0, sp_t, ALU.max, ALU.add))
                precise_exp(v, st, sp_s[:, 0:16], a_neg, sp_t[:, 0:16], sp_k[:, 0:16].bitcast(I32))
                stt(da, dtk[:, :, :], -1.0, sp_s[:, 0:16].unsqueeze(1).to_broadcast([P, 3, 16]),
                    ALU.mult, ALU.mult).then_inc(da_ready.sem, da_ready.up())
                dve.wait_ge(da_ready.sem, da_ready.at(1))
                for i, src in enumerate((dtk, da)):
                    v.tensor_copy(wide_dt[:, i].rearrange("b (h q) -> b h q", q=64),
                                  src[0:TS, 2, :].unsqueeze(2).to_broadcast([TS, 16, 64])).then_inc(da_ready.sem, da_ready.up())
                for n in range(4):
                    c, j = n // 2, n % 2
                    dve.wait_ge(xtok_done.sem, xtok_done.at(n + 1))
                    tt(xdt[:, c, 512 * j:512 * j + 512].rearrange("p (h q) -> p h q", q=64),
                       ps[:, n, :].rearrange("p (h q) -> p h q", q=64),
                       dtk[:, c, 8 * j:8 * j + 8].unsqueeze(2).to_broadcast([P, 8, 64]), ALU.mult).then_inc(xtok_taken.sem, xtok_taken.up())
                dve.wait_ge(xtok_done.sem, xtok_done.at(6))
                tt(Gm, ps[:, 5, :].rearrange("p (j l) -> p j l", j=4),
                   tri[:, :].unsqueeze(1).to_broadcast([P, 4, P]), ALU.mult).then_inc(gm_taken.sem, gm_taken.up())
                dve.wait_ge(cum_done.sem, cum_done.at(1))
                st(v.tensor_copy(acum, ps[:, 6, 0:32].rearrange("p (c n) -> p c n", c=2)))
                st(v.tensor_copy(cdec, ps[:, 6, 32:64].rearrange("p (c n) -> p c n", c=2)))
                tt(dend, cdec, acum, ALU.subtract).then_inc(cum_taken.sem, cum_taken.up())
                dve.wait_ge(spread_done.sem, spread_done.at(1))
                v.tensor_copy(dexp, ps[:, 7, 0:128].rearrange("p (k i b) -> p k i b", k=8, i=2)).then_inc(spread_taken.sem, spread_taken.up())
                dve.wait_ge(ends_ready.sem, ends_ready.at(1))
                dve.wait_ge(xtok_taken.sem, xtok_taken.at(4))
                for n in range(4):
                    c, g = n // 2, n % 2
                    tt(xw[:, c, 512 * g:512 * g + 512].rearrange("p (h q) -> p h q", q=64),
                       xdt[:, c, 512 * g:512 * g + 512].rearrange("p (h q) -> p h q", q=64),
                       dend[:, c, 8 * g:8 * g + 8].unsqueeze(2).to_broadcast([P, 8, 64]), ALU.mult).then_inc(xw_ready.sem, xw_ready.up())

                def segments(n):
                    c, qd = n // 4, n % 4
                    dve.wait_ge(row_done.sem, row_done.at(n + 1))
                    if n >= 2:
                        dve.wait_ge(m_ready.sem, m_ready.at(n - 1))
                    for j in range(4):
                        hd = 4 * qd + j
                        ins = ts(seg[:, n % 2, j * P:(j + 1) * P], ps[:, 4 + n % 2, j * P:(j + 1) * P],
                                 acum[:, c, hd:hd + 1], 0.0, ALU.subtract, ALU.min)
                    ins.then_inc(seg_ready.sem, seg_ready.up())

                def masked(n):
                    c, qd = n // 4, n % 4
                    g = qd // 2
                    dve.wait_ge(seg_exp.sem, seg_exp.at((n + 1) + max(0, n - 3)))
                    if n >= 2:
                        dve.wait_ge(ysd_done.sem, ysd_done.at(n - 1))
                    four = lambda a: a.rearrange("p (j l) -> p j l", j=4)
                    if c:
                        tt(four(CE[:, n % 2, :]), four(rowexp[:, n % 2, :]),
                           xbc[:, 10 + g, c * P:(c + 1) * P].unsqueeze(1).to_broadcast([P, 4, P]), ALU.mult)
                    dve.wait_ge(gm_taken.sem, gm_taken.at(1))
                    tt(four(Mt[:, n % 2, :]), four(seg[:, n % 2, :]),
                       Gm[:, 2 * c + g, :].unsqueeze(1).to_broadcast([P, 4, P]), ALU.mult).then_inc(m_ready.sem, m_ready.up())

                def take_y(n):
                    c, qd = n // 4, n % 4
                    dve.wait_ge(ysd_done.sem, ysd_done.at(n + 1))
                    for j in range(2):
                        k = 2 * qd + j
                        x = xbc[:, k, c * P:(c + 1) * P]
                        stt(x, x, m2_dc[:, k:k + 1], ps[:, 6 + n % 2, j * P:(j + 1) * P],
                            ALU.mult, ALU.add).then_inc(ysd_taken.sem, ysd_taken.up())

                segments(0)
                segments(1)
                for n in range(2):
                    dve.wait_ge(st_done.sem, st_done.at(n + 1))
                    v.tensor_copy(S0[:, 512 * n:512 * n + 512], ps[:, n, :]).then_inc(st_taken.sem, st_taken.up())
                for n in range(8):
                    masked(n)
                    if n + 2 < 8:
                        segments(n + 2)
                    if n == 1:
                        dve.wait_ge(st_taken.sem, st_taken.at(2))
                        st(tt(fin.rearrange("p (h q) -> p h q", q=64), S0.rearrange("p (h q) -> p h q", q=64),
                              cdec[:, 1, :].unsqueeze(2).to_broadcast([P, 16, 64]), ALU.mult))
                        for g in range(2):
                            dve.wait_ge(st_done.sem, st_done.at(3 + g))
                            tt(fin[:, 512 * g:512 * g + 512], fin[:, 512 * g:512 * g + 512],
                               ps[:, 2 + g, :], ALU.add).then_inc(st_taken.sem, st_taken.up())
                    if n >= 1:
                        take_y(n - 1)
                take_y(7)
                for n in range(2):
                    dve.wait_ge(fin_tr.sem, fin_tr.at(n + 1))
                    v.tensor_copy(fout[:, 512 * n:512 * n + 512], ps[:, n, :]).then_inc(fin_taken.sem, fin_taken.up())
                dve.wait_ge(spread_taken.sem, spread_taken.at(1))
                st(tt(xds, xbc[:, 0:8, TP:T], dexp[:, :, 0, :], ALU.mult))
                for b in range(TS):
                    dve.wait_ge(bc_done.sem, bc_done.at(b + 1))
                    dve.wait_ge(carried_scaled.sem, carried_scaled.at(8 * (b + 1)))
                    for k in range(8):
                        o = hs[:, b % 2, k, :]
                        st_ = stt(o, ps[:, 2 + b % 2, (k // 4) * P:(k // 4 + 1) * P], xds[:, k, b:b + 1], o,
                                  ALU.mult, ALU.add)
                    st(st_)
                    for k in range(8):
                        ins = v.tensor_tensor_reduce(
                            junk, hs[:, b % 2, k, :], ps[:, 2 + b % 2, (2 + k // 4) * P:(3 + k // 4) * P], 1.0, 0.0,
                            ALU.mult, ALU.add, ys[:, k, b:b + 1])
                        if k < 7:
                            st(ins)
                    ins.then_inc(bc_taken.sem, bc_taken.up())
                    dve.wait_ge(bc_taken.sem, bc_taken.at(b + 1))
                for k in range(8):
                    x = xbc[:, k, TP:T]
                    ins = stt(x, x, m2_dc[:, k:k + 1], ys[:, k, :], ALU.mult, ALU.add)
                st(ins)
                tt(z, z, xbc[:, 0:8, :], ALU.mult)

            @block.scalar
            def _(act):
                act.wait_ge(xtok_done.sem, xtok_done.at(5))
                nc.scalar.copy(Btok.rearrange("p j n -> p (j n)"), ps[:, 4, :]).then_inc(btok_taken.sem, btok_taken.up())
                act.wait_ge(cum_taken.sem, cum_taken.at(1))
                nc.scalar.activation(cdec, cdec, ACT.Exp)
                nc.scalar.activation(dend, dend, ACT.Exp).then_inc(ends_ready.sem, ends_ready.up())
                act.wait_ge(spread_taken.sem, spread_taken.at(1))
                nc.scalar.activation(dexp[:, :, 1, :], dexp[:, :, 1, :], ACT.Exp).then_inc(spread_taken.sem, spread_taken.up())
                for n in range(8):
                    act.wait_ge(seg_ready.sem, seg_ready.at(n + 1))
                    if n >= 4:
                        if n >= 6:
                            act.wait_ge(m_ready.sem, m_ready.at(n - 1))
                        nc.scalar.activation(rowexp[:, n % 2, :], ps[:, 4 + n % 2, :], ACT.Exp).then_inc(seg_exp.sem, seg_exp.up())
                    nc.scalar.activation(seg[:, n % 2, :], seg[:, n % 2, :], ACT.Exp).then_inc(seg_exp.sem, seg_exp.up())
                act.wait_ge(spread_taken.sem, spread_taken.at(2))
                for b in range(TS):
                    act.wait_ge(carried_in[b % 2].sem, carried_in[b % 2].at(16 * (b // 2 + 1)))
                    for k in range(8):
                        o = hs[:, b % 2, k, :]
                        nc.scalar.activation(o, o, ACT.Copy, scale=dexp[:, k, 1, b:b + 1]).then_inc(carried_scaled.sem, carried_scaled.up())
        Signal.stage()

        sig = A[:, 0:8 * T].rearrange("p (k t) -> p k t", t=T)
        sq_m2 = A[:, 8 * T:16 * T].rearrange("p (k t) -> p k t", t=T)
        sq_s5 = xbc[:, 0:8, :]
        gelu_ready, glu_done, sig_ready, gated = (signal(s) for s in (
            "gelu_ready", "glu_block_done", "gate_ready", "gated_block_ready"))
        with nc.Block() as block:
            @block.sync
            def _(sp):
                load_through(sp, 36)

            @block.scalar
            def _(act):
                for k in range(8):
                    nc.scalar.activation(u[:, k, :], u[:, k, :], ACT.Gelu_apprx_tanh).then_inc(gelu_ready.sem, gelu_ready.up())
                norm_act(act, z, sq_m2, 8, T)
                for o in range(8):
                    act.wait_ge(glu_done.sem, glu_done.at(o + 1))
                    nc.scalar.activation(sig[:, o, :], ps[:, o % 7, 0:T], ACT.Sigmoid,
                                         bias=glu_bc[:, o:o + 1]).then_inc(sig_ready.sem, sig_ready.up())
                act.wait_ge(normed.sem, normed.at(8))
                norm_act(act, xn, sq_s5, 8, T, source=gated)

            @block.tensor
            def _(pe):
                pe.wait_ge(gelu_ready.sem, gelu_ready.at(8))
                for o in range(8):
                    if o == 0 or o == 4:
                        pe.wait_ge(*loaded(G["glu"][0] + o // 4))
                    if o == 7:
                        pe.wait_ge(sig_ready.sem, sig_ready.at(1))
                    w = slot(G["glu"][0] + o // 4).rearrange("p (k n) -> p k n", n=512)
                    for k in range(8):
                        mm = nc.tensor.matmul(ps[:, o % 7, 0:T], w[:, k, (o % 4) * P:(o % 4 + 1) * P], u[:, k, :],
                                              start=(k == 0), stop=(k == 7))
                        if k == 7:
                            mm.then_inc(glu_done.sem, glu_done.up())
                    if o == 3:
                        norm_pe(pe, sq_m2, 8, T, 0)
                        pe.wait_ge(glu_done.sem, glu_done.at(4))
                        pe.sem_inc(slab_used.sem, 1)
                        slab_used.n += 1
                pe.wait_ge(glu_done.sem, glu_done.at(8))
                pe.sem_inc(slab_used.sem, 1)
                slab_used.n += 1
                pe.wait_ge(root_ready.sem, root_ready.at(1))
                norm_pe(pe, sq_s5, 8, T, 8)

            @block.vector
            def _(dve):
                norm_dve(dve, z, xn[:, 8:16, :], m2_wc, 8, T, 1)
                for o in range(8):
                    dve.wait_ge(sig_ready.sem, sig_ready.at(o + 1))
                    nc.vector.tensor_tensor(xn[:, o, :], sig[:, o, :], u[:, o, :], ALU.mult).then_inc(gated.sem, gated.up())
                norm_dve(dve, xn, xn, s5_wc, 8, T, 2)
        Signal.stage()

        sqA = A[:, :].rearrange("p (k t) -> p k t", t=T)

        def project_add_norm(name, w, load_to):
            with nc.Block() as block:
                @block.sync
                def _(sp):
                    first, n = G[name]
                    load_matrix_loop(sp, name, first + n)
                    load_through(sp, load_to)

                @block.tensor
                def _(pe):
                    project_pe(pe, name)
                    pe.wait_ge(block_taken.sem, block_taken.at(16 + 8))
                    norm_pe(pe, sqA, KB, T, 0)

                @block.scalar
                def _(act):
                    norm_act(act, XT, sqA, KB, T, source=block_taken, ahead=8)

                @block.vector
                def _(dve):
                    def take(k, b):
                        x = XT[:, bass.ds(k, 1), :]
                        return nc.vector.tensor_tensor(x, x, ps[:, b:b + 1, 0:T], ALU.add)
                    project_take(dve, name, take)
                    norm_dve(dve, XT, xn, w, KB, T, 1)
            Signal.stage()

        project_add_norm("w_out", w_xa, 44)

        Q = h[:, 0:16, :]
        with nc.Block() as block:
            @block.sync
            def _(sp):
                load_matrix_loop(sp, "xa_wq", 48)
                load_through(sp, 52)

            @block.tensor
            def _(pe):
                project_pe(pe, "xa_wq")

            @block.vector
            def _(dve):
                project_take(dve, "xa_wq", lambda k, b: nc.vector.tensor_copy(
                    h[:, bass.ds(k, 1), :], ps[:, b:b + 1, 0:T]))
        Signal.stage()

        SCALE = float(DX) ** -0.5
        Pm = A[:, 0:2048].rearrange("p (j m) -> p j m", m=MEM)
        PT = A[:, 2048:4096].rearrange("p (a j l) -> p a j l", a=2, l=P)
        st8 = A[:, 4096:4224]
        nmax, rsum = st8[:, 0:8], st8[:, 8:16]
        wide8 = H[:, 16 * T:28 * T]
        sS = wide8[:, 0:64].rearrange("p (a j) -> p a j", a=2)
        sP = wide8[0:32, 64:320]
        sPT = wide8[:, 320:384].rearrange("p (a j) -> p a j", a=2)
        snm, ssum = wide8[0:32, 384:385], wide8[0:32, 385:386]
        junk8 = wide8[:, 512:1024]
        (sc_done, max_ready, exp8, norm8, pt_done, pt_taken, pv_done, pv_taken, qrow_done, sscore,
         st_tr, st_trt, smax_ready, sexp_ready, so_done, so_taken) = (signal(f"att_{n}") for n in (
             "scores_done", "max_ready", "exp_ready", "weights_ready", "weights_transposed",
             "weights_transpose_taken", "output_done", "output_taken", "query_rows_done", "sample_scores_ready",
             "sample_transposed", "sample_transpose_taken", "sample_max_ready", "sample_exp_ready",
             "sample_output_done", "sample_output_taken"))
        with nc.Block() as block:
            @block.sync
            def _(sp):
                load_through(sp, 68)

            @block.tensor
            def _(pe):
                for j in range(8):
                    hd, a = j // 2, j % 2
                    for d in range(4):
                        mm = nc.tensor.matmul(ps[:, j // 2, a * MEM:(a + 1) * MEM],
                                              Q[:, 4 * hd + d, a * P:(a + 1) * P], KT[:, 4 * hd + d, :],
                                              start=(d == 0), stop=(d == 3))
                mm.then_inc(sc_done.sem, sc_done.up())

                def query_rows(b):
                    first = 4 if b % 2 == 0 else 0
                    if b >= 2:
                        pe.wait_ge(sscore.sem, sscore.at(8 * (b - 1)))
                    elif b == 1:
                        pe.wait_ge(pv_taken.sem, pv_taken.at(8))
                    for k in range(KB):
                        mm = nc.tensor.matmul(ps[:, first + k // 4, (k % 4) * P:(k % 4 + 1) * P],
                                              Q[:, k, TP + b:TP + b + 1].to_broadcast([P, P]), ident[:, :],
                                              start=True, stop=True)
                    mm.then_inc(qrow_done.sem, qrow_done.up())

                query_rows(0)
                for n in range(4):
                    a, j0 = n // 2, 4 * (n % 2)
                    pe.wait_ge(norm8.sem, norm8.at(8))
                    for j in range(j0, j0 + 4):
                        mm = nc.tensor.transpose(ps[:, n, (j - j0) * P:(j - j0 + 1) * P],
                                                 Pm[:, j, a * P:(a + 1) * P], ident[:, :])
                    mm.then_inc(pt_done.sem, pt_done.up())
                for k in range(KB):
                    hd = k // 4
                    if k == 0:
                        pe.wait_ge(pt_taken.sem, pt_taken.at(4))
                    if k >= 8 and k % 2 == 0:
                        pe.wait_ge(pv_taken.sem, pv_taken.at(k // 2 - 3))
                    for a in range(2):
                        mm = nc.tensor.matmul(ps[:, k // 2 % 4, (k % 2) * TP:(k % 2 + 1) * TP],
                                              V[:, a, k * P:(k + 1) * P],
                                              PT[:, a, 2 * hd:2 * hd + 2, :].rearrange("p j l -> p (j l)"),
                                              start=(a == 0), stop=(a == 1))
                    if k % 2:
                        mm.then_inc(pv_done.sem, pv_done.up())
                for b in range(1, TS):
                    query_rows(b)
                pe.wait_ge(sscore.sem, sscore.at(8 * TS))
                for a in range(2):
                    mm = nc.tensor.transpose(ps[0:32, 4, a * P:(a + 1) * P], sS[:, a, :], ident[:, :])
                mm.then_inc(st_tr.sem, st_tr.up())
                pe.wait_ge(sexp_ready.sem, sexp_ready.at(2))
                for a in range(2):
                    mm = nc.tensor.transpose(ps[:, 5, 32 * a:32 * a + 32], sP[:, a * P:(a + 1) * P],
                                             ident[0:32, 0:32])
                mm.then_inc(st_tr.sem, st_tr.up())
                pe.wait_ge(st_trt.sem, st_trt.at(1))
                for b in range(TS):
                    g = G["values"][0] + b
                    pe.wait_ge(*loaded(g))
                    vb = slot(g).rearrange("p (a n) -> p a n", a=2)
                    for k in range(KB):
                        for a in range(2):
                            mm = nc.tensor.matmul(ps[:, 6, TS * k + b:TS * k + b + 1], vb[:, a, k * P:(k + 1) * P],
                                                  sPT[:, a, 4 * b + k // 4:4 * b + k // 4 + 1],
                                                  start=(a == 0), stop=(a == 1))
                    mm.then_inc(slab_used.sem, slab_used.up())

            @block.vector
            def _(dve):
                st = stepper(dve, "dve")
                v = nc.vector
                dve.wait_ge(sc_done.sem, sc_done.at(1))
                st(v.tensor_reduce(nmax, ps[:, 0:4, :].rearrange("p b (a m) -> p (b a) m", a=2), AX.X, ALU.max))
                v.tensor_scalar(nmax, nmax, -SCALE, None, ALU.mult).then_inc(max_ready.sem, max_ready.up())
                dve.wait_ge(exp8.sem, exp8.at(8))
                st(v.reciprocal(rsum, rsum))
                for j in range(8):
                    v.tensor_scalar(Pm[:, j, :], Pm[:, j, :], rsum[:, j:j + 1], None, ALU.mult).then_inc(norm8.sem, norm8.up())
                for b in range(TS):
                    g = G["keys"][0] + b
                    first = 4 if b % 2 == 0 else 0
                    dve.wait_ge(*loaded(g))
                    dve.wait_ge(qrow_done.sem, qrow_done.at(b + 1))
                    kb = slot(g).rearrange("p (a n) -> p a n", a=2)
                    for a in range(2):
                        for hd in range(HX):
                            n = 8 * b + 4 * a + hd
                            if n:
                                dve.wait_ge(sscore.sem, sscore.at(n))
                            v.tensor_tensor_reduce(
                      junk8, kb[:, a, DX * hd:DX * (hd + 1)], ps[:, first + hd, :], 1.0, 0.0,
                      ALU.mult, ALU.add, sS[:, a, 4 * b + hd:4 * b + hd + 1]).then_inc(sscore.sem, sscore.up())
                    dve.wait_ge(sscore.sem, sscore.at(8 * (b + 1)))
                    dve.sem_inc(key_slab_used.sem, 1)
                    key_slab_used.n += 1
                dve.wait_ge(st_tr.sem, st_tr.at(1))
                st(v.tensor_reduce(snm, ps[0:32, 4, 0:256], AX.X, ALU.max))
                v.tensor_scalar(snm, snm, -SCALE, None, ALU.mult).then_inc(smax_ready.sem, smax_ready.up())
                dve.wait_ge(sexp_ready.sem, sexp_ready.at(1))
                st(v.reciprocal(ssum, ssum))
                v.tensor_scalar(sP, sP, ssum, None, ALU.mult).then_inc(sexp_ready.sem, sexp_ready.up())
                dve.wait_ge(st_tr.sem, st_tr.at(2))
                v.tensor_copy(sPT, ps[:, 5, 0:64].rearrange("p (a j) -> p a j", a=2)).then_inc(st_trt.sem, st_trt.up())
                dve.wait_ge(*used(G["values"][0] + TS - 1))
                v.tensor_copy(xn[:, :, TP:T], ps[:, 6, 0:KB * TS].rearrange("p (k b) -> p k b", b=TS))

            @block.scalar
            def _(act):
                act.wait_ge(max_ready.sem, max_ready.at(1))
                for j in range(8):
                    nc.scalar.activation(Pm[:, j, :], ps[:, j // 2, (j % 2) * MEM:(j % 2 + 1) * MEM],
                                         ACT.Exp, bias=nmax[:, j:j + 1], scale=SCALE,
                                         accum_out=rsum[:, j:j + 1]).then_inc(exp8.sem, exp8.up())
                for n in range(4):
                    a, j0 = n // 2, 4 * (n % 2)
                    act.wait_ge(pt_done.sem, pt_done.at(n + 1))
                    nc.scalar.copy(PT[:, a, j0:j0 + 4, :].rearrange("p j l -> p (j l)"), ps[:, n, :]).then_inc(pt_taken.sem, pt_taken.up())
                for n in range(8):
                    act.wait_ge(pv_done.sem, pv_done.at(n + 1))
                    nc.scalar.copy(xn[:, 2 * n:2 * n + 2, 0:TP],
                                   ps[:, n % 4, :].rearrange("p (k t) -> p k t", k=2)).then_inc(pv_taken.sem, pv_taken.up())
                act.wait_ge(smax_ready.sem, smax_ready.at(1))
                nc.scalar.activation(sP, ps[0:32, 4, 0:256], ACT.Exp, bias=snm, scale=SCALE,
                                     accum_out=ssum).then_inc(sexp_ready.sem, sexp_ready.up())
        Signal.stage()

        project_add_norm("xa_wo", w_ffn, 76)

        rw = A[:, 0:576].rearrange("p (k n) -> p k n", n=36)
        lg = A[:, 576:684].rearrange("p (a n) -> p a n", n=36)
        rt = A[:, 1024:2048]
        gT = A[0:32, 2048:2048 + T]
        gates_tok = A[:, 2400:2496].rearrange("p (a g j) -> p a g j", a=3, g=GROUPS_X)
        Gb = M[:, 0:EXPERTS * T].rearrange("p (e t) -> p e t", t=T)
        (rw_in, lg_done, r_exp, r_arg, gate_ready, gt_done, gt_taken, gb_done, gb_taken) = (
            signal(f"router_{n}") for n in ("weights_loaded", "logits_done", "exp_ready", "argument_ready",
                                            "gates_ready", "gates_transposed", "gates_transpose_taken",
                                            "gates_spread", "gates_spread_taken"))
        with nc.Block() as block:
            @block.sync
            def _(sp):
                sp.dma_start(rw[:, :, 0:4], by_rows(I["router_coarse_w"][0])).then_inc(rw_in.sem, rw_in.up(16))
                sp.dma_start(rw[:, :, 4:36], by_rows(I["router_fine_w"][0])).then_inc(rw_in.sem, rw_in.up(16))

            @block.tensor
            def _(pe):
                pe.wait_ge(rw_in.sem, rw_in.at(32))
                for a in range(3):
                    n = P if a < 2 else TS
                    for k in range(KB):
                        mm = nc.tensor.matmul(ps[0:n, 0, 36 * a:36 * a + 36], xn[:, k, a * P:a * P + n],
                                              rw[:, k, :], start=(k == 0), stop=(k == KB - 1))
                mm.then_inc(lg_done.sem, lg_done.up())
                pe.wait_ge(gate_ready.sem, gate_ready.at(1))
                for a in range(3):
                    n = P if a < 2 else TS
                    mm = nc.tensor.transpose(ps[0:32, 1, a * P:a * P + n],
                                             gates_tok[0:n, a].rearrange("p g j -> p (g j)"), ident[0:n, 0:n])
                mm.then_inc(gt_done.sem, gt_done.up())
                pe.wait_ge(gt_taken.sem, gt_taken.at(1))
                for e in range(EXPERTS):
                    if e >= 4:
                        pe.wait_ge(gb_taken.sem, gb_taken.at(e - 3))
                    nc.tensor.matmul(ps[:, 2 + e % 4, 0:T], ident[0:32, e:e + 1].to_broadcast([32, P]),
                                     gT, start=True, stop=True).then_inc(gb_done.sem, gb_done.up())

            @block.scalar
            def _(act):
                act.wait_ge(r_arg.sem, r_arg.at(1))
                nc.scalar.activation(rt[:, 0:12], rt[:, 0:12], ACT.Exp).then_inc(r_exp.sem, r_exp.up())
                act.wait_ge(r_arg.sem, r_arg.at(2))
                nc.scalar.activation(rt[:, 96:99], rt[:, 96:99], ACT.Exp).then_inc(r_exp.sem, r_exp.up())

            @block.vector
            def _(dve):
                st = stepper(dve, "dve")
                v = nc.vector
                tt = v.tensor_tensor
                three = lambda lo, n: rt[:, lo:lo + 3 * n].rearrange("p (a n) -> p a n", a=3)
                ce, cm, ohg, rank, t24, m = three(0, 4), three(12, 1), three(16, 4), three(32, 8), three(256, 8), \
                    three(60, 1)
                lf, oh1, oh2, m1, m2, e2 = three(128, 8), three(160, 8), three(192, 8), three(90, 1), \
                    three(93, 1), three(96, 1)
                g1, g2, gc = three(100, 1), three(104, 1), three(108, 1)
                big = rt[:, 300:396].rearrange("p (a g j) -> p a g j", a=3, g=GROUPS_X)

                def wide(x, n):
                    return x.to_broadcast([P, 3, n])

                def first_max(out, x, mx, n, scratch):
                    st(v.tensor_reduce(mx, x, AX.X, ALU.max))
                    st(tt(out, x, wide(mx, n), ALU.is_equal))
                    st(tt(out, out, rank[:, :, 0:n], ALU.mult))
                    st(v.tensor_reduce(m, out, AX.X, ALU.max))
                    st(tt(out, out, wide(m, n), ALU.is_equal))

                st(v.memset(lg, 0.0))
                for i in range(8):
                    ins = v.memset(rank[:, :, i:i + 1], 8.0 - i)
                st(ins)
                dve.wait_ge(lg_done.sem, lg_done.at(1))
                st(tt(lg[:, 0:2, :], ps[:, 0, 0:72].rearrange("p (a n) -> p a n", a=2),
                      r_b.unsqueeze(1).to_broadcast([P, 2, 36]), ALU.add))
                st(tt(lg[0:TS, 2, :], ps[0:TS, 0, 72:108], r_b[0:TS, :], ALU.add))
                first_max(ohg, lg[:, :, 0:4], cm, 4, None)
                tt(ce, lg[:, :, 0:4], wide(cm, 4), ALU.subtract).then_inc(r_arg.sem, r_arg.up())
                fine = lg[:, :, 4:36].rearrange("p a (g j) -> p a g j", g=GROUPS_X)
                for a in range(3):
                    ins = tt(big[:, a], fine[:, a], ohg[:, a, :].unsqueeze(2).to_broadcast([P, 4, 8]), ALU.mult)
                st(ins)
                st(tt(lf, big[:, :, 0, :], big[:, :, 1, :], ALU.add))
                st(tt(lf, lf, big[:, :, 2, :], ALU.add))
                st(tt(lf, lf, big[:, :, 3, :], ALU.add))
                first_max(oh1, lf, m1, 8, None)
                st(v.scalar_tensor_tensor(t24, oh1, -3.0e38, lf, ALU.mult, ALU.add))
                first_max(oh2, t24, m2, 8, None)
                tt(e2, m2, m1, ALU.subtract).then_inc(r_arg.sem, r_arg.up())
                dve.wait_ge(r_exp.sem, r_exp.at(1))
                st(v.tensor_reduce(gc, ce, AX.X, ALU.add))
                dve.wait_ge(r_exp.sem, r_exp.at(2))
                st(v.tensor_scalar(g1, e2, 1.0, None, ALU.add))
                st(tt(g1, g1, gc, ALU.mult))
                st(v.reciprocal(g1, g1))
                st(tt(g2, g1, e2, ALU.mult))
                st(tt(oh1, oh1, wide(g1, 8), ALU.mult))
                st(tt(oh2, oh2, wide(g2, 8), ALU.mult))
                st(tt(oh1, oh1, oh2, ALU.add))
                for a in range(3):
                    ins = tt(gates_tok[:, a], oh1[:, a, :].unsqueeze(1).to_broadcast([P, 4, 8]),
                             ohg[:, a, :].unsqueeze(2).to_broadcast([P, 4, 8]), ALU.mult)
                ins.then_inc(gate_ready.sem, gate_ready.up())
                dve.wait_ge(gt_done.sem, gt_done.at(1))
                v.tensor_copy(gT, ps[0:32, 1, 0:T]).then_inc(gt_taken.sem, gt_taken.up())
                for e in range(EXPERTS):
                    dve.wait_ge(gb_done.sem, gb_done.at(e + 1))
                    v.tensor_copy(Gb[:, e, :], ps[:, 2 + e % 4, 0:T]).then_inc(gb_taken.sem, gb_taken.up())
        Signal.stage()

        mid = H[:, 0:8 * T].rearrange("p (s j t) -> p s j t", s=2, t=T)
        sg = H[:, 8 * T:12 * T].rearrange("p (s j t) -> p s j t", s=2, t=T)
        silu_ready, half_done, mid_ready, down_done, down_taken, sg_gated, gated_s = (
            signal(f"moe_{n}") for n in ("silu_ready", "half_done", "middle_ready", "down_block_done",
                                         "down_block_taken", "silu_buffer_free", "silu_gated"))
        M0 = G["moe"][0]
        TURNS, PAIRS = EXPERTS // 4, 2

        def used_in_turn(i, it):
            return used(M0 + i, it * 12)

        with nc.Block() as block:
            @block.sync
            def _(sp):
                with sp.Fori(0, TURNS - 1) as it:
                    for i in range(NS, 12 + NS):
                        e, which = PAIR[i % 6]
                        sp.wait_ge(*used(M0 + i - NS, it * 12))
                        src = expert_slab(it * 4 + (2 * (i // 6) + e), which)
                        sp.dma_start(slab_view(M0 + i, which), src).then_inc(slab_loaded[(M0 + i) % NS].sem, 16)
                for i in range(NS):
                    slab_loaded[i].n += 16 * 3 * (TURNS - 1)
                loaded_to[0] += 12 * (TURNS - 1)
                load_through(sp, M0 + 3 * EXPERTS)

            @block.tensor
            def _(pe):
                with pe.Fori(0, TURNS) as it:
                    for i in range(12):
                        pair, (e, which) = i // 6, PAIR[i % 6]
                        g = M0 + i
                        ex = 2 * pair + e
                        if which < 2:
                            pe.wait_ge(*loaded(g, it * 48))
                            w = slab_view(g, which)
                            for f in range(2):
                                if f == 0:
                                    if which == 0:
                                        pe.wait_ge(silu_ready.sem, silu_ready.at(2 * ex + 2 + it * 8))
                                    else:
                                        pe.wait_ge(mid_ready.sem, mid_ready.at(ex + 1 + it * 4))
                                for k in range(KB):
                                    mm = nc.tensor.matmul(ps[:, 2 * which + f, 0:T], w[:, k, f * P:(f + 1) * P],
                                                          xn[:, k, :], start=(k == 0), stop=(k == KB - 1))
                                    if k == KB - 1:
                                        mm.then_inc((half_done if f == 0 else slab_used).sem, 1)
                        elif e == 0:
                            pe.wait_ge(*loaded(g, it * 48))
                            pe.wait_ge(*loaded(g + 1, it * 48))
                            ws = [slab_view(g, 2), slab_view(g + 1, 2)]
                            for d4 in range(4):
                                for ee in range(2):
                                    if d4 == 0:
                                        pe.wait_ge(mid_ready.sem, mid_ready.at(2 * pair + ee + 2 + it * 4))
                                    for d in range(4 * d4, 4 * d4 + 4):
                                        if ee == 0:
                                            pe.wait_ge(down_taken.sem, down_taken.at(16 * pair + d + 1 + it * 32))
                                        for f in range(2):
                                            mm = nc.tensor.matmul(
                                                ps[:, 4 + d % 4, 0:T], ws[ee][:, f, d * P:(d + 1) * P],
                                                mid[:, pair, 2 * ee + f, :],
                                                start=(ee == 0 and f == 0), stop=(ee == 1 and f == 1))
                                            if ee and d < 15 and f:
                                                mm.then_inc(down_done.sem, 1)
                                            if ee and d == 15:
                                                mm.then_inc(slab_used.sem, 1)
                slab_used.n += 3 * EXPERTS

            @block.scalar
            def _(act):
                act.sem_inc(silu_ready.sem, 2)
                with act.Fori(0, TURNS) as it:
                    for ex in range(4):
                        i = 6 * (ex // 2) + 2 * (ex % 2)
                        for f in range(2):
                            if f == 0:
                                act.wait_ge(half_done.sem, half_done.at(2 * ex + 1 + it * 8))
                                act.wait_ge(sg_gated.sem, sg_gated.at(ex + 1 + it * 4))
                            else:
                                act.wait_ge(*used_in_turn(i, it))
                            nc.scalar.activation(sg[:, ex % 2, f, :], ps[:, f, 0:T], ACT.Silu).then_inc(
                                silu_ready.sem, 1)

            @block.vector
            def _(dve):
                v = nc.vector
                dve.sem_inc(sg_gated.sem, 2)
                dve.sem_inc(mid_ready.sem, 1)
                dve.sem_inc(down_taken.sem, 4)

                def middle(ex, it):
                    pair, e = ex // 2, ex % 2
                    s = sg[:, ex % 2]
                    dve.wait_ge(silu_ready.sem, silu_ready.at(2 * ex + 4 + it * 8))
                    gate = Gb[:, bass.ds(it * 4 + ex, 1), :].to_broadcast([P, 2, T])
                    v.tensor_tensor(s, s, gate, ALU.mult).then_inc(gated_s.sem, 1)
                    dve.wait_ge(gated_s.sem, gated_s.at(ex + 1 + it * 4))
                    dve.wait_ge(*used_in_turn(6 * pair + 2 * e + 1, it))
                    v.tensor_tensor(mid[:, pair, 2 * e:2 * e + 2, :], s, ps[:, 2:4, 0:T], ALU.mult).then_inc(
                        mid_ready.sem, 1)

                with dve.Fori(0, TURNS) as it:
                    for pair in range(2):
                        for e in range(2):
                            ex = 2 * pair + e
                            middle(ex, it)
                            dve.wait_ge(mid_ready.sem, mid_ready.at(ex + 2 + it * 4))
                            dve.sem_inc(sg_gated.sem, 1)
                        for d in range(16):
                            if d < 15:
                                dve.wait_ge(down_done.sem, down_done.at(15 * pair + d + 1 + it * 30))
                            else:
                                dve.wait_ge(*used_in_turn(6 * pair + 5, it))
                            v.tensor_tensor(XT[:, d, :], XT[:, d, :], ps[:, 4 + d % 4, 0:T],
                                            ALU.add).then_inc(down_taken.sem, 1)
        silu_ready.n += 2 * EXPERTS + 2
        down_taken.n += 16 * EXPERTS // 2 + 4
        Signal.stage()

        yrows = M[:, 0:6144].rearrange("p (a n) -> p a n", a=3)
        out_done, out_taken, out_stored = signal("rows_done"), signal("rows_taken"), signal("outputs_stored")
        with nc.Block() as block:
            @block.scalar
            def _(act):
                norm_act(act, XT, sqA, KB, T)

            @block.tensor
            def _(pe):
                norm_pe(pe, sqA, KB, T, 0)
                for n in range(12):
                    a, k4 = n % 3, n // 3
                    rows = P if a < 2 else TS
                    pe.wait_ge(normed.sem, normed.at(4 * k4 + 4))
                    if n >= 7:
                        pe.wait_ge(out_taken.sem, out_taken.at(n - 6))
                    for k in range(4 * k4, 4 * k4 + 4):
                        mm = nc.tensor.transpose(ps[0:rows, n % 7, (k % 4) * P:(k % 4 + 1) * P],
                                                 xn[:, k, a * P:a * P + rows], ident[:, :])
                    mm.then_inc(out_done.sem, out_done.up())

            @block.vector
            def _(dve):
                norm_dve(dve, XT, xn, w_fin, KB, T, 1)
                for n in range(12):
                    a, k4 = n % 3, n // 3
                    rows = P if a < 2 else TS
                    dve.wait_ge(out_done.sem, out_done.at(n + 1))
                    nc.vector.tensor_copy(yrows[0:rows, a, 512 * k4:512 * k4 + 512],
                                          ps[0:rows, n % 7, :]).then_inc(out_taken.sem, out_taken.up())

            @block.sync
            def _(sp):
                sp.wait_ge(out_taken.sem, out_taken.at(12))
                sp.dma_start(O["y_prompt"][0].rearrange("(a p) n -> p a n", p=P), yrows[:, 0:2, :]).then_inc(out_stored.sem, out_stored.up(16))
                sp.dma_start(O["y_sample"].rearrange("b s n -> (b s) n"), yrows[0:TS, 2, :]).then_inc(out_stored.sem, out_stored.up(16))
                sp.wait_ge(out_stored.sem, out_stored.at(32))


OUTPUTS = [("y_prompt", (1, TP, D)), ("y_sample", (TS, 1, D)), ("p_s5_re", (1, 1, 64, 64)),
           ("p_s5_im", (1, 1, 64, 64)), ("p_ssm", (1, 1, 16, 64, 128)), ("p_conv", (1, 1, 3, 1536)),
           ("p_mem_k", (1, 1, MEM, HX, DX)), ("p_mem_v", (1, 1, MEM, HX, DX)), ("s_s5_re", (1, TS, 64, 64)),
           ("s_s5_im", (1, TS, 64, 64)), ("s_ssm", (1, TS, 16, 64, 128)), ("s_conv", (1, TS, 3, 1536))]


def kernel(**inputs):
    import numpy as np
    import concourse.bacc as bacc
    from concourse.bass_utils import run_bass_kernel_spmd

    nc = bacc.Bacc("TRN2", target_bir_lowering=False, num_devices=1)
    arrays, ins = {}, {}
    for name, a in inputs.items():
        a = np.ascontiguousarray(a)
        arrays[f"in_{name}"] = a
        ins[name] = nc.dram_tensor(f"in_{name}", a.shape, mybir.dt.from_np(a.dtype), kind="ExternalInput").ap()
    outs = {name: nc.dram_tensor(f"out_{name}", shape, F32, kind="ExternalOutput").ap()
            for name, shape in OUTPUTS}
    build(nc, ins, outs)
    r = run_bass_kernel_spmd(nc, [arrays], core_ids=[0])
    return tuple(r.results[0][f"out_{name}"] for name, _ in OUTPUTS)
```
